# Optimizing a Trainium2 kernel written in Bass

```python
import jax, jax.numpy as jnp
from jax import lax
import numpy as np

D_MODEL = 2048
BATCH = 1
SEQ = 256
DEPTH = 1

EPS = 1e-6
N_BRANCH = 3
CONV_WIDTH = D_MODEL
CONV_K = 3
SB_HEAD_DIM = 128
SB_HEADS = D_MODEL // SB_HEAD_DIM
SB_WIDTH = SB_HEADS * SB_HEAD_DIM
Q_BLOCK = 128
SSD_EXPAND = 2
SSD_WIDTH = SSD_EXPAND * D_MODEL
SSD_HEAD_DIM = 64
SSD_HEADS = SSD_WIDTH // SSD_HEAD_DIM
SSD_GROUPS = 8
SSD_HPG = SSD_HEADS // SSD_GROUPS
SSD_STATE = 128
SSD_CONV_K = 4
SSD_CHUNK = 128
SSD_XBC = SSD_WIDTH + 2 * SSD_GROUPS * SSD_STATE
SSD_IN = SSD_WIDTH + SSD_XBC + SSD_HEADS
A_IN = 3 * CONV_WIDTH
B_IN = 3 * SB_WIDTH
G_IN = N_BRANCH * D_MODEL
IN_PROJ_WIDTH = A_IN + B_IN + SSD_IN + G_IN
PEER_HEADS = 8
PEER_NKEYS = 128
PEER_EXPERTS = PEER_NKEYS * PEER_NKEYS
PEER_TOPK = 16
PEER_DK = 256
PEER_TOKEN_BLOCK = 128

kernel_name = "hybrid_conv_stickbreak_ssd_peer"

def rmsnorm(x, w):
    xf = x.astype(jnp.float32)
    y = xf * lax.rsqrt(jnp.mean(xf * xf, axis=-1, keepdims=True) + EPS)
    return (y * w.astype(jnp.float32)).astype(x.dtype)

def causal_depthwise_conv(x, w, b=None):
    k_width, chans = w.shape
    y = lax.conv_general_dilated(
        x, w[:, None, :].astype(x.dtype), window_strides=(1,),
        padding=[(k_width - 1, 0)], dimension_numbers=('NWC', 'WIO', 'NWC'),
        feature_group_count=chans)
    return y if b is None else y + b.astype(x.dtype)

def short_conv_mixer(u, conv_w):
    b_gate, c_gate, hid = jnp.split(u, 3, axis=-1)
    return b_gate * causal_depthwise_conv(c_gate * hid, conv_w)

def stick_breaking_attention(u):
    q, k, v = jnp.split(u, 3, axis=-1)
    bsz, seq, _ = q.shape
    q = q.reshape(bsz, seq, SB_HEADS, SB_HEAD_DIM)
    k = k.reshape(bsz, seq, SB_HEADS, SB_HEAD_DIM)
    v = v.reshape(bsz, seq, SB_HEADS, SB_HEAD_DIM)
    scale = SB_HEAD_DIM ** -0.5
    key_pos = jnp.arange(seq)

    def block(i):
        start = i * Q_BLOCK
        qb = lax.dynamic_slice_in_dim(q, start, Q_BLOCK, axis=1)
        z = jnp.einsum('bthd,bshd->bhts', qb, k, preferred_element_type=jnp.float32) * scale
        q_pos = start + jnp.arange(Q_BLOCK)
        mask = key_pos[None, :] < q_pos[:, None]
        log_not_beta = jnp.where(mask, jax.nn.log_sigmoid(-z), 0.0)
        later = lax.cumsum(log_not_beta, axis=3, reverse=True) - log_not_beta
        a = jnp.where(mask, jnp.exp(jax.nn.log_sigmoid(z) + later), 0.0)
        return jnp.einsum('bhts,bshd->bthd', a.astype(v.dtype), v)

    o = lax.map(block, jnp.arange(seq // Q_BLOCK))
    return o.transpose(1, 0, 2, 3, 4).reshape(bsz, seq, SB_WIDTH)

def segsum_exp(a):
    length = a.shape[-1]
    cs = jnp.cumsum(a, axis=-1)
    diff = cs[..., :, None] - cs[..., None, :]
    mask = jnp.tril(jnp.ones((length, length), dtype=bool))
    return jnp.where(mask, jnp.exp(jnp.where(mask, diff, 0.0)), 0.0)

def mamba2_ssd(u, conv_w, conv_b, dt_bias, a_log, d_skip, norm_w):
    bsz, seq, _ = u.shape
    nc = seq // SSD_CHUNK
    z, xbc, dt = jnp.split(u, [SSD_WIDTH, SSD_WIDTH + SSD_XBC], axis=-1)
    xbc = jax.nn.silu(causal_depthwise_conv(xbc, conv_w, conv_b))
    xs, bm, cm = jnp.split(xbc, [SSD_WIDTH, SSD_WIDTH + SSD_GROUPS * SSD_STATE], axis=-1)
    xs = xs.astype(jnp.float32).reshape(bsz, nc, SSD_CHUNK, SSD_GROUPS, SSD_HPG, SSD_HEAD_DIM)
    bm = bm.astype(jnp.float32).reshape(bsz, nc, SSD_CHUNK, SSD_GROUPS, SSD_STATE)
    cm = cm.astype(jnp.float32).reshape(bsz, nc, SSD_CHUNK, SSD_GROUPS, SSD_STATE)
    dt = jax.nn.softplus(dt.astype(jnp.float32) + dt_bias.astype(jnp.float32))
    a = -jnp.exp(a_log.astype(jnp.float32))
    dt_c = dt.reshape(bsz, nc, SSD_CHUNK, SSD_GROUPS, SSD_HPG)
    da = (dt_c * a.reshape(SSD_GROUPS, SSD_HPG)).transpose(0, 3, 4, 1, 2)
    xdt = xs * dt_c[..., None]
    a_cs = jnp.cumsum(da, axis=-1)
    cb = jnp.einsum('bclgn,bcsgn->bgcls', cm, bm)
    y_diag = jnp.einsum('bgcls,bgrcls,bcsgrp->bclgrp', cb, segsum_exp(da), xdt)
    decay_to_end = jnp.exp(a_cs[..., -1:] - a_cs)
    states = jnp.einsum('bclgn,bgrcl,bclgrp->bcgrpn', bm, decay_to_end, xdt)
    chunk_decay = jnp.exp(a_cs[..., -1])

    def step(hs, inp):
        s_c, d_c = inp
        return hs * d_c[..., None, None] + s_c, hs

    h0 = jnp.zeros((bsz, SSD_GROUPS, SSD_HPG, SSD_HEAD_DIM, SSD_STATE), jnp.float32)
    _, prev = lax.scan(step, h0, (states.transpose(1, 0, 2, 3, 4, 5), chunk_decay.transpose(3, 0, 1, 2)))
    y_off = jnp.einsum('bclgn,cbgrpn,bgrcl->bclgrp', cm, prev, jnp.exp(a_cs))
    y = y_diag + y_off + xs * d_skip.astype(jnp.float32).reshape(SSD_GROUPS, SSD_HPG)[:, :, None]
    y = y.reshape(bsz, seq, SSD_WIDTH)
    yg = (y * jax.nn.silu(z.astype(jnp.float32))).reshape(bsz, seq, SSD_GROUPS, -1)
    yg = yg * lax.rsqrt(jnp.mean(yg * yg, axis=-1, keepdims=True) + EPS)
    return (yg.reshape(bsz, seq, SSD_WIDTH) * norm_w.astype(jnp.float32)).astype(u.dtype)

def hybrid_mixer(n, w_in, conv_a_w, ssd_conv_w, ssd_conv_b, ssd_dt_bias, ssd_a_log, ssd_d,
                 ssd_norm_w, w_branch_a, w_branch_b, w_branch_c, w_out):
    u = n @ w_in
    u_a, u_b, u_c, u_g = jnp.split(u, [A_IN, A_IN + B_IN, A_IN + B_IN + SSD_IN], axis=-1)
    y_a = short_conv_mixer(u_a, conv_a_w) @ w_branch_a
    y_b = stick_breaking_attention(u_b) @ w_branch_b
    y_c = mamba2_ssd(u_c, ssd_conv_w, ssd_conv_b, ssd_dt_bias, ssd_a_log, ssd_d, ssd_norm_w) @ w_branch_c
    g_a, g_b, g_c = jnp.split(jax.nn.sigmoid(u_g), 3, axis=-1)
    return (g_a * y_a + g_b * y_b + g_c * y_c) @ w_out

def peer_ffn(n, w_query, sub_keys, expert_down, expert_up):
    bsz, seq, dm = n.shape
    ntok = bsz * seq
    nt = n.reshape(ntok, dm)
    q = (nt @ w_query).reshape(ntok, PEER_HEADS, 2, PEER_DK // 2)
    s = jnp.einsum('thcd,hcnd->thcn', q, sub_keys, preferred_element_type=jnp.float32)
    s1, i1 = lax.top_k(s[:, :, 0], PEER_TOPK)
    s2, i2 = lax.top_k(s[:, :, 1], PEER_TOPK)
    cand_s = (s1[..., :, None] + s2[..., None, :]).reshape(ntok, PEER_HEADS, PEER_TOPK * PEER_TOPK)
    cand_i = (i1[..., :, None] * PEER_NKEYS + i2[..., None, :]).reshape(ntok, PEER_HEADS, PEER_TOPK * PEER_TOPK)
    top_s, pos = lax.top_k(cand_s, PEER_TOPK)
    idx = jnp.take_along_axis(cand_i, pos, axis=-1)
    gate = jax.nn.softmax(top_s, axis=-1)
    nb = ntok // PEER_TOKEN_BLOCK
    hk = PEER_HEADS * PEER_TOPK

    def block(args):
        xb, ib, gb = args
        down = expert_down[ib]
        act = jax.nn.gelu(jnp.einsum('td,tkd->tk', xb, down), approximate=False)
        up = expert_up[ib]
        return jnp.einsum('tk,tkd->td', gb.astype(xb.dtype) * act, up)

    out = lax.map(block, (nt.reshape(nb, PEER_TOKEN_BLOCK, dm),
                          idx.reshape(nb, PEER_TOKEN_BLOCK, hk),
                          gate.reshape(nb, PEER_TOKEN_BLOCK, hk)))
    return out.reshape(bsz, seq, dm)

def setup_inputs(seed: int = 0) -> dict:
    key = jax.random.key(seed)
    ks = jax.random.split(key, 24)
    f32 = jnp.float32

    def nrm(k, shape, scale):
        return jax.random.normal(k, shape, f32) * scale

    dt0 = jnp.exp(jax.random.uniform(ks[8], (DEPTH, SSD_HEADS), f32, np.log(1e-3), np.log(1e-1)))
    return {
        "x": nrm(ks[0], (BATCH, SEQ, D_MODEL), 1.0),
        "norm_mix_w": 1.0 + nrm(ks[1], (DEPTH, D_MODEL), 0.02),
        "w_in": nrm(ks[2], (DEPTH, D_MODEL, IN_PROJ_WIDTH), D_MODEL ** -0.5),
        "conv_a_w": nrm(ks[3], (DEPTH, CONV_K, CONV_WIDTH), CONV_K ** -0.5),
        "ssd_conv_w": nrm(ks[4], (DEPTH, SSD_CONV_K, SSD_XBC), SSD_CONV_K ** -0.5),
        "ssd_conv_b": nrm(ks[5], (DEPTH, SSD_XBC), 0.01),
        "ssd_dt_bias": dt0 + jnp.log(-jnp.expm1(-dt0)),
        "ssd_a_log": jnp.log(jax.random.uniform(ks[6], (DEPTH, SSD_HEADS), f32, 1.0, 16.0)),
        "ssd_d": 1.0 + nrm(ks[7], (DEPTH, SSD_HEADS), 0.02),
        "ssd_norm_w": 1.0 + nrm(ks[9], (DEPTH, SSD_WIDTH), 0.02),
        "w_branch_a": nrm(ks[10], (DEPTH, CONV_WIDTH, D_MODEL), CONV_WIDTH ** -0.5),
        "w_branch_b": nrm(ks[11], (DEPTH, SB_WIDTH, D_MODEL), SB_WIDTH ** -0.5),
        "w_branch_c": nrm(ks[12], (DEPTH, SSD_WIDTH, D_MODEL), SSD_WIDTH ** -0.5),
        "w_out": nrm(ks[13], (DEPTH, D_MODEL, D_MODEL), D_MODEL ** -0.5),
        "norm_ffn_w": 1.0 + nrm(ks[14], (DEPTH, D_MODEL), 0.02),
        "peer_w_query": nrm(ks[15], (DEPTH, D_MODEL, PEER_HEADS * PEER_DK), D_MODEL ** -0.5),
        "peer_sub_keys": nrm(ks[16], (DEPTH, PEER_HEADS, 2, PEER_NKEYS, PEER_DK // 2), (PEER_DK // 2) ** -0.5),
        "peer_down": nrm(ks[17], (DEPTH, PEER_EXPERTS, D_MODEL), D_MODEL ** -0.5),
        "peer_up": nrm(ks[18], (DEPTH, PEER_EXPERTS, D_MODEL), PEER_HEADS ** -0.5),
        "final_norm_w": 1.0 + nrm(ks[19], (D_MODEL,), 0.02),
    }

def reference(x, norm_mix_w, w_in, conv_a_w, ssd_conv_w, ssd_conv_b, ssd_dt_bias, ssd_a_log,
              ssd_d, ssd_norm_w, w_branch_a, w_branch_b, w_branch_c, w_out, norm_ffn_w,
              peer_w_query, peer_sub_keys, peer_down, peer_up, final_norm_w):
    h = x
    for l in range(DEPTH):
        h = h + hybrid_mixer(rmsnorm(h, norm_mix_w[l]), w_in[l], conv_a_w[l], ssd_conv_w[l],
                             ssd_conv_b[l], ssd_dt_bias[l], ssd_a_log[l], ssd_d[l], ssd_norm_w[l],
                             w_branch_a[l], w_branch_b[l], w_branch_c[l], w_out[l])
        h = h + peer_ffn(rmsnorm(h, norm_ffn_w[l]), peer_w_query[l], peer_sub_keys[l],
                         peer_down[l], peer_up[l])
    return rmsnorm(h, final_norm_w)


_drawn_inputs = setup_inputs


def setup_inputs(seed=0):
    import zlib

    import numpy as np

    out = dict(_drawn_inputs(seed))
    spreads = {}
    factors = {'ssd_conv_b': 4.419,
     'ssd_d': 4.491,
     'ssd_norm_w': 3.581,
     'norm_ffn_w': 2.725,
     'final_norm_w': 2.914}
    for name, (base, spread) in spreads.items():
        noise = np.random.default_rng([zlib.crc32(name.encode()), seed]).standard_normal(out[name].shape)
        drawn = base * np.exp(spread * noise) if base else spread * noise
        out[name] = __import__('jax').numpy.asarray(drawn.astype(out[name].dtype))
    for name, factor in factors.items():
        out[name] = (out[name] * factor).astype(out[name].dtype)
    return out
```

```python
import numpy as np
import concourse.bass as bass
from concourse import mybir
from contextlib import ExitStack

F32 = mybir.dt.float32
F32R = mybir.dt.float32r
U32 = mybir.dt.uint32
ALU = mybir.AluOpType
ACT = mybir.ActivationFunctionType
AX = mybir.AxisListType
ds = bass.ds

P = 128
D = 2048
T = 256
TB = T // P
KD = D // P
EPS = 1e-6
SBH = 16
SCALE = 128.0 ** -0.5
SSD_W = 4096
GROUPS = 8
HPG = 8
SSD_HEADS = 64
KC = SSD_W // P
COL_A = 0
COL_B = 3 * D
COL_Z = 6 * D
COL_XS = COL_Z + SSD_W
COL_BM = COL_XS + SSD_W
COL_CM = COL_BM + GROUPS * P
COL_DT = COL_CM + GROUPS * P
COL_G = COL_DT + SSD_HEADS
V_NORM = 0
V_FFN = 16
V_CONVA = 32
V_CONVB = 80
V_SSDW = 128
V_SSDN = 320
NEG = -30000.0
PH, PK, PN = 8, 16, 128


def program(nc, x, norm_mix_w, w_in, conv_a_w, ssd_conv_w, ssd_conv_b, ssd_dt_bias, ssd_a_log, ssd_d,
            ssd_norm_w, w_branch_a, w_branch_b, w_branch_c, w_out, norm_ffn_w, peer_w_query,
            peer_sub_keys, peer_down, peer_up, final_norm_w, out):
    top = ExitStack()
    with top:
        def sb(ctx, name, shape, dt=F32):
            return ctx.enter_context(nc.sbuf_tensor(name, shape, dt))

        live = []

        def sem(name):
            live.append(nc.alloc_semaphore(name=name))
            return live[-1]

        bank = [top.enter_context(nc.psum_tensor(f"bank{i}", [P, 512], F32)) for i in range(8)]

        ident = sb(top, "ident", [P, P])
        vcols = sb(top, "vcols", [P, 352])
        eps_col = sb(top, "eps_col", [P, 1])

        class Stream:

            def __init__(self, ctx, tag, cols, units, pieces):
                self.units, self.pieces = units, pieces
                self.raw = [sb(ctx, f"{tag}_raw{i}", [P, cols]) for i in range(4)]
                self.hi = [sb(ctx, f"{tag}_hi{i}", [P, cols], F32R) for i in range(2)]
                self.lo = [sb(ctx, f"{tag}_lo{i}", [P, cols], F32R) for i in range(2)]
                self.raw_full = [sem(f"{tag}_raw_full{i}") for i in range(4)]
                self.hi_done = sem(f"{tag}_hi_done")
                self.lo_done = sem(f"{tag}_lo_done")
                self.unit_used = sem(f"{tag}_unit_used")

            def load(self, sp, it, u, first, pairs):
                if not (first and u < 4):
                    sp.wait_ge(self.lo_done, it * self.units + u - 3)
                for dst, src in pairs:
                    sp.dma_start(dst, src).then_inc(self.raw_full[u % 4], 16)

            def split_hi(self, act, it, u, first, cols):
                act.wait_ge(self.raw_full[u % 4], (it * (self.units // 4) + u // 4 + 1) * (16 * self.pieces))
                if not (first and u < 2):
                    act.wait_ge(self.unit_used, it * self.units + u - 1)
                nc.scalar.activation(self.hi[u % 2][:, 0:cols], self.raw[u % 4][:, 0:cols],
                                     ACT.Copy).then_inc(self.hi_done, 1)

            def split_lo(self, dve, it, u, cols):
                dve.wait_ge(self.hi_done, it * self.units + u + 1)
                nc.vector.tensor_tensor(self.lo[u % 2][:, 0:cols], self.raw[u % 4][:, 0:cols],
                                        self.hi[u % 2][:, 0:cols].bitcast(F32),
                                        ALU.subtract).then_inc(self.lo_done, 1)

            def wait_unit(self, pe, it, u):
                pe.wait_ge(self.lo_done, it * self.units + u + 1)

        def tri_matmul(out, lhs, rhs, start, stop):
            nc.tensor.matmul(out, lhs[0], rhs[0], start=start, stop=False, skip_group_check=True)
            nc.tensor.matmul(out, lhs[0], rhs[1], start=False, stop=False, skip_group_check=True)
            return nc.tensor.matmul(out, lhs[1], rhs[0], start=False, stop=stop, skip_group_check=True)

        acc = sb(top, "acc", [P, TB, D])
        mix = ExitStack()
        with mix:
            xT_hi = sb(mix, "xT_hi", [P, KD, T], F32R)
            xT_lo = sb(mix, "xT_lo", [P, KD, T], F32R)
            yT_hi = sb(mix, "yT_hi", [P, KC, T], F32R)
            yT_lo = sb(mix, "yT_lo", [P, KC, T], F32R)

            c = ExitStack()
            with c:
                xt = sb(c, "xt", [P, TB, D])
                junk = sb(c, "junk", [P, D])
                vrows = sb(c, "vrows", [P, 3, P])
                rstd = sb(c, "rstd", [P, TB])
                std = sb(c, "std", [P, TB])
                ssq = sb(c, "ssq", [P, TB])
                p_const = sem("p_const")
                p_vec_in = sem("p_vec_in")
                p_x_in = [sem(f"p_x_in{i}") for i in range(2)]
                p_ssq = sem("p_ssq")
                p_std = sem("p_std")
                p_rstd = sem("p_rstd")
                p_scaled = sem("p_scaled")
                p_vecT = sem("p_vecT")
                p_vcols = sem("p_vcols")
                p_xT = sem("p_xT")
                p_hi = sem("p_hi")
                p_lo = sem("p_lo")
                with nc.Block() as block:
                    @block.sync
                    def _(sp):
                        for tb in range(TB):
                            sp.dma_start(xt[:, tb, :], x[0, tb * P:(tb + 1) * P, :]).then_inc(p_x_in[tb], 16)
                        rows = lambda a, n: a.rearrange("k (c p) -> (k c) p", p=P)
                        cw = ssd_conv_w[0].rearrange("k (c p) -> k c p", p=P)
                        for dst, src in (
                            (vrows[0:16, 0, :], rows(norm_mix_w, 16)),
                            (vrows[16:32, 0, :], rows(norm_ffn_w, 16)),
                            (vrows[80:128, 0, :], rows(ssd_conv_b, 48)),
                            (vrows[64:96, 2, :], rows(ssd_norm_w, 32)),
                            *((vrows[32 + 16 * k:48 + 16 * k, 0, :],
                               conv_a_w[0, k:k + 1, :].rearrange("o (c p) -> (o c) p", p=P)) for k in range(3)),
                            (vrows[0:48, 1, :], cw[0]), (vrows[48:96, 1, :], cw[1]),
                            (vrows[96:128, 1, :], cw[2, 0:32]), (vrows[0:16, 2, :], cw[2, 32:48]),
                            (vrows[16:64, 2, :], cw[3]),
                        ):
                            sp.dma_start(dst, src).then_inc(p_vec_in, 16)

                    @block.gpsimd
                    def _(pool):
                        pool.memset(ident[:, :], 0.0).then_inc(p_const, 1)
                        pool.memset(eps_col[:, :], EPS).then_inc(p_const, 1)
                        pool.wait_ge(p_const, 2)
                        pool.affine_select(out=ident[:, :], in_=ident[:, :], compare_op=ALU.not_equal, fill=1.0,
                                           base=0, pattern=[[-1, P]], channel_multiplier=1).then_inc(p_const, 1)

                    @block.scalar
                    def _(act):
                        act.wait_ge(p_const, 2)
                        for tb in range(TB):
                            act.wait_ge(p_x_in[tb], 16)
                            if tb:
                                act.wait_ge(p_ssq, tb)
                            nc.scalar.activation(junk[:, :], xt[:, tb, :], ACT.Square,
                                                 accum_out=ssq[:, tb:tb + 1]).then_inc(p_ssq, 1)
                        act.wait_ge(p_ssq, TB)
                        nc.scalar.activation(std[:, :], ssq[:, :], ACT.Sqrt, bias=eps_col[:, 0:1],
                                             scale=1.0 / D).then_inc(p_std, 1)
                        act.wait_ge(p_vcols, 1)
                        for k in range(KD):
                            act.wait_ge(p_xT, 2 * (k // 2) + 2)
                            nc.scalar.activation(xT_hi[:, k, :], bank[k // 2][:, (k % 2) * T:(k % 2 + 1) * T],
                                                 ACT.Copy, scale=vcols[:, V_NORM + k:V_NORM + k + 1]).then_inc(p_hi, 1)

                    @block.vector
                    def _(dve):
                        dve.wait_ge(p_vecT, 1)
                        nc.vector.tensor_copy(vcols[:, 0:256], bank[0][:, 0:256])
                        nc.vector.tensor_copy(vcols[:, 256:352], bank[0][:, 256:352]).then_inc(p_vcols, 1)
                        dve.wait_ge(p_std, 1)
                        nc.vector.reciprocal(rstd[:, :], std[:, :]).then_inc(p_rstd, 1)
                        dve.wait_ge(p_rstd, 1)
                        for tb in range(TB):
                            nc.vector.tensor_scalar(xt[:, tb, :], xt[:, tb, :], rstd[:, tb:tb + 1], None,
                                                    ALU.mult).then_inc(p_scaled, 1)
                        for k in range(KD):
                            dve.wait_ge(p_hi, 2 * (k // 2) + 2)
                            nc.vector.scalar_tensor_tensor(
                                out=xT_lo[:, k, :], in0=bank[k // 2][:, (k % 2) * T:(k % 2 + 1) * T],
                                scalar=vcols[:, V_NORM + k:V_NORM + k + 1], in1=xT_hi[:, k, :].bitcast(F32),
                                op0=ALU.mult, op1=ALU.subtract).then_inc(p_lo, 1)

                    @block.tensor
                    def _(pe):
                        pe.wait_ge(p_const, 3)
                        pe.wait_ge(p_vec_in, 16 * 12)
                        nc.tensor.transpose(bank[0][:, 0:128], vrows[:, 0, :], ident[:, :])
                        nc.tensor.transpose(bank[0][:, 128:256], vrows[:, 1, :], ident[:, :])
                        nc.tensor.transpose(bank[0][:, 256:352], vrows[0:96, 2, :], ident[0:96, 0:96]).then_inc(p_vecT, 1)
                        pe.wait_ge(p_vcols, 1)
                        pe.wait_ge(p_scaled, TB)
                        for k in range(KD):
                            for tb in range(TB):
                                at = (k % 2) * T + tb * P
                                last = nc.tensor.transpose(bank[k // 2][:, at:at + P],
                                                           xt[:, tb, k * P:(k + 1) * P], ident[:, :])
                            last.then_inc(p_xT, 1)

            c = ExitStack()
            with c:
                W = 768
                st = Stream(c, "a", 2 * W, 8, 3)
                N_IT = 8
                c_sb = sb(c, "a_c", [P, 512])
                b_sb = sb(c, "a_b", [P, 512])
                gate_hid = sb(c, "a_gate_hid", [P, 2, T + 2])
                y_f = sb(c, "a_y", [P, 2, T])
                a_pad = sem("a_pad")
                a_evac = sem("a_evac")
                a_gh = sem("a_gh")
                a_conv = sem("a_conv")
                a_y = sem("a_y_done")
                a_yhi = sem("a_yhi")
                a_ylo = sem("a_ylo")
                with nc.Block() as block:
                    @block.sync
                    def _(sp):
                        def body(it, first):
                            for u in range(8):
                                raw = st.raw[u % 4][:, :].rearrange("p (k n) -> p k n", k=2)
                                st.load(sp, it, u, first, [
                                    (raw[:, :, i * 256:(i + 1) * 256],
                                     w_in[0, u * 256:(u + 1) * 256, ds(COL_A + i * D + it * 256, 256)].rearrange(
                                         "(k p) n -> p k n", p=P)) for i in range(3)])
                        body(0, True)
                        with sp.Fori(1, N_IT) as it:
                            body(it, False)

                    @block.scalar
                    def _(act):
                        def evacuate(p):
                            act.wait_ge(st.unit_used, 8 * p + 8)
                            nc.scalar.activation(c_sb[:, :], bank[1][:, :], ACT.Copy).then_inc(a_evac, 1)
                            nc.scalar.activation(b_sb[:, :], bank[0][:, :], ACT.Copy).then_inc(a_evac, 1)

                        def y_hi(p):
                            act.wait_ge(a_y, p + 1)
                            nc.scalar.activation(yT_hi[:, ds(2 * p, 2), :], y_f[:, :, :], ACT.Copy).then_inc(a_yhi, 1)

                        def body(it, first):
                            for u in range(8):
                                st.split_hi(act, it, u, first, 2 * W)
                                if not first and u == 0:
                                    evacuate(it - 1)
                                if not first and u == 4:
                                    y_hi(it - 1)
                        body(0, True)
                        with act.Fori(1, N_IT) as it:
                            body(it, False)
                        evacuate(N_IT - 1)
                        y_hi(N_IT - 1)

                    @block.gpsimd
                    def _(pool):
                        pool.memset(gate_hid[:, :, :], 0.0).then_inc(a_pad, 1)

                    @block.vector
                    def _(dve):
                        def gate(p):
                            if isinstance(p, int) and p == 0:
                                dve.wait_ge(a_pad, 1)
                            dve.wait_ge(a_evac, 2 * p + 1)
                            nc.vector.tensor_tensor(gate_hid[:, :, 2:T + 2],
                                                    c_sb[:, :].rearrange("p (j t) -> p j t", j=2),
                                                    bank[2][:, :].rearrange("p (j t) -> p j t", j=2),
                                                    ALU.mult).then_inc(a_gh, 1)

                        def conv(p, j):
                            if j == 0:
                                dve.wait_ge(a_gh, p + 1)
                            w = lambda k: vcols[:, ds(V_CONVA + 16 * k + 2 * p + j, 1)]
                            nc.vector.tensor_scalar(y_f[:, j, :], gate_hid[:, j, 2:T + 2], w(2), None,
                                                    ALU.mult).then_inc(a_conv, 1)
                            for k in (1, 0):
                                dve.wait_ge(a_conv, 6 * p + 3 * j + 2 - k)
                                nc.vector.scalar_tensor_tensor(
                                    out=y_f[:, j, :], in0=gate_hid[:, j, k:k + T], scalar=w(k), in1=y_f[:, j, :],
                                    op0=ALU.mult, op1=ALU.add).then_inc(a_conv, 1)

                        def y(p):
                            dve.wait_ge(a_conv, 6 * p + 6)
                            dve.wait_ge(a_evac, 2 * p + 2)
                            nc.vector.tensor_tensor(y_f[:, :, :], y_f[:, :, :],
                                                    b_sb[:, :].rearrange("p (j t) -> p j t", j=2),
                                                    ALU.mult).then_inc(a_y, 1)

                        def y_lo(p):
                            dve.wait_ge(a_yhi, p + 1)
                            nc.vector.tensor_tensor(yT_lo[:, ds(2 * p, 2), :], y_f[:, :, :],
                                                    yT_hi[:, ds(2 * p, 2), :].bitcast(F32),
                                                    ALU.subtract).then_inc(a_ylo, 1)

                        def body(it, p):
                            for u in range(8):
                                if it is not None:
                                    st.split_lo(dve, it, u, 2 * W)
                                if p is None:
                                    continue
                                if u == 0:
                                    gate(p)
                                if u in (1, 2):
                                    conv(p, u - 1)
                                if u == 3:
                                    y(p)
                                if u == 6:
                                    y_lo(p)
                        body(0, None)
                        body(1, 0)
                        with dve.Fori(2, N_IT) as it:
                            body(it, it - 1)
                        body(None, N_IT - 1)

                    @block.tensor
                    def _(pe):
                        def body(it, first):
                            if not first:
                                pe.wait_ge(a_evac, 2 * it)
                                pe.wait_ge(a_gh, it)
                            for u in range(8):
                                st.wait_unit(pe, it, u)
                                for kk in range(2):
                                    k = 2 * u + kk
                                    for m in range(6):
                                        at = slice(kk * W + m * P, kk * W + (m + 1) * P)
                                        last = tri_matmul(bank[m // 2][:, (m % 2) * T:(m % 2 + 1) * T],
                                                          (st.hi[u % 2][:, at], st.lo[u % 2][:, at]),
                                                          (xT_hi[:, k, :], xT_lo[:, k, :]),
                                                          start=k == 0 and m % 2 == 0, stop=k == KD - 1)
                                last.then_inc(st.unit_used, 1)
                        body(0, True)
                        with pe.Fori(1, N_IT) as it:
                            body(it, False)

            def branch(tag, gate_col, w_branch, kb, y0):
                c = ExitStack()
                with c:
                    UN, N_IT = 4 + kb // 4, D // 512
                    add = tag != "ga"
                    st = Stream(c, tag, 4 * 512, UN, 2)
                    sig = sb(c, tag + "_sig", [P, TB, 512])
                    gated = sb(c, tag + "_gated", [P, TB, 512])
                    sig_done = sem(tag + "_sig_done")
                    gated_done = sem(tag + "_gated_done")
                    added = sem(tag + "_added")
                    with nc.Block() as block:
                        @block.sync
                        def _(sp):
                            def body(it, first):
                                for u in range(UN):
                                    raw = st.raw[u % 4][:, :].rearrange("p (k n) -> p k n", k=4)
                                    part = (lambda r: w_in[0, u * 512 + r:u * 512 + r + 256, ds(gate_col + it * 512, 512)]) \
                                        if u < 4 else \
                                        (lambda r: w_branch[0, (u - 4) * 512 + r:(u - 4) * 512 + r + 256, ds(it * 512, 512)])
                                    st.load(sp, it, u, first, [
                                        (raw[:, half * 2:half * 2 + 2, :],
                                         part(half * 256).rearrange("(k p) n -> p k n", p=P)) for half in (1, 0)])
                            body(0, True)
                            with sp.Fori(1, N_IT) as it:
                                body(it, False)

                        @block.scalar
                        def _(act):
                            def body(it, first):
                                for u in range(UN):
                                    st.split_hi(act, it, u, first, 2048)
                                    if u == 5:
                                        act.wait_ge(st.unit_used, it * UN + 4)
                                        if not first:
                                            act.wait_ge(gated_done, 2 * it)
                                        for tb in range(TB):
                                            nc.scalar.activation(sig[:, tb, :], bank[tb][:, :],
                                                                 ACT.Sigmoid).then_inc(sig_done, 1)
                            body(0, True)
                            with act.Fori(1, N_IT) as it:
                                body(it, False)

                        @block.vector
                        def _(dve):
                            def gate(p):
                                dve.wait_ge(st.unit_used, p * UN + UN)
                                dve.wait_ge(sig_done, 2 * p + 2)
                                for tb in range(TB):
                                    dst = gated[:, tb, :] if add else acc[:, tb, ds(p * 512, 512)]
                                    nc.vector.tensor_tensor(dst, sig[:, tb, :], bank[2 + tb][:, :],
                                                            ALU.mult).then_inc(gated_done, 1)
                                if add:
                                    dve.wait_ge(gated_done, 2 * p + 2)
                                    here = acc[:, :, ds(p * 512, 512)]
                                    nc.vector.tensor_tensor(here, here, gated[:, :, :], ALU.add).then_inc(added, 1)

                            def body(it, p):
                                for u in range(UN):
                                    if it is not None:
                                        st.split_lo(dve, it, u, 2048)
                                    if p is not None and u == 0:
                                        gate(p)
                            body(0, None)
                            body(1, 0)
                            with dve.Fori(2, N_IT) as it:
                                body(it, it - 1)
                            gate(N_IT - 1)

                        @block.tensor
                        def _(pe):
                            def body(it, first):
                                for u in range(UN):
                                    if u == 0 and not first:
                                        pe.wait_ge(sig_done, 2 * it)
                                    if u == 4 and not first:
                                        pe.wait_ge(gated_done, 2 * it)
                                    st.wait_unit(pe, it, u)
                                    for kk in range(4):
                                        k = 4 * u + kk if u < 4 else 4 * (u - 4) + kk
                                        at = slice(kk * 512, (kk + 1) * 512)
                                        for tb in range(TB):
                                            t = slice(tb * P, (tb + 1) * P)
                                            lhs = ((xT_hi[:, k, t], xT_lo[:, k, t]) if u < 4 else
                                                   (yT_hi[:, y0 + k, t], yT_lo[:, y0 + k, t]))
                                            last = tri_matmul(bank[tb + (2 if u >= 4 else 0)][:, :], lhs,
                                                              (st.hi[u % 2][:, at], st.lo[u % 2][:, at]),
                                                              start=k == 0,
                                                              stop=k == (KD if u < 4 else kb) - 1)
                                    last.then_inc(st.unit_used, 1)
                            body(0, True)
                            with pe.Fori(1, N_IT) as it:
                                body(it, False)

            branch("ga", COL_G, w_branch_a, KD, 0)

            c = ExitStack()
            with c:
                W = 768
                UN, N_IT, PA = 8, 8, 3 * P
                st = Stream(c, "b", 2 * W, UN, 3)
                q_sb = sb(c, "b_q", [P, 2, T])
                k_sb = sb(c, "b_k", [P, 2, T])
                v_sb = sb(c, "b_v", [P, TB, 2 * P])
                mask = sb(c, "b_mask", [P, PA])
                mask_neg = sb(c, "b_mask_neg", [P, PA])
                neg_tri = sb(c, "b_neg_tri", [P, P])
                neg_one = sb(c, "b_neg_one", [P, P])
                z_abs = sb(c, "b_z_abs", [P, 2, PA])
                z_exp = sb(c, "b_z_exp", [P, 2, PA])
                z_ln = sb(c, "b_z_ln", [P, 2, PA])
                splus = sb(c, "b_splus", [P, 2, PA])
                expo = sb(c, "b_expo", [P, 2, PA])
                a_sb = sb(c, "b_a", [P, 2, PA])
                b_const = sem("b_const")
                b_qk = sem("b_qk_copied")
                b_v = sem("b_v_copied")
                b_z = sem("b_z")
                b_abs = sem("b_abs")
                b_e = sem("b_e")
                b_ln = sem("b_ln")
                b_sp1 = sem("b_sp1")
                b_sp = sem("b_sp")
                b_cum = sem("b_cum")
                b_expo = sem("b_expo_done")
                b_a = sem("b_a_done")
                b_o = sem("b_o")
                b_ohi = sem("b_ohi")
                b_olo = sem("b_olo")
                Q, K_, V, Z, O_ = bank[0], bank[1], bank[2], (bank[3], bank[4]), bank[5]
                with nc.Block() as block:
                    @block.sync
                    def _(sp):
                        def body(it, first):
                            for u in range(UN):
                                raw = st.raw[u % 4][:, :].rearrange("p (k n) -> p k n", k=2)
                                st.load(sp, it, u, first, [
                                    (raw[:, :, i * 256:(i + 1) * 256],
                                     w_in[0, u * 256:(u + 1) * 256, ds(COL_B + i * D + it * 256, 256)].rearrange(
                                         "(k p) n -> p k n", p=P)) for i in range(3)])
                        body(0, True)
                        with sp.Fori(1, N_IT) as it:
                            body(it, False)

                    @block.gpsimd
                    def _(pool):
                        pool.memset(mask[:, :], 1.0).then_inc(b_const, 1)
                        pool.memset(mask_neg[:, :], 0.0).then_inc(b_const, 1)
                        pool.memset(neg_tri[:, :], -1.0).then_inc(b_const, 1)
                        pool.memset(neg_one[:, :], -1.0).then_inc(b_const, 1)
                        pool.wait_ge(b_const, 4)
                        for at in (0, 2 * P):
                            for m, fill in ((mask, 0.0), (mask_neg, NEG)):
                                pool.affine_select(out=m[:, at:at + P], in_=m[:, at:at + P], compare_op=ALU.is_ge,
                                                   fill=fill, base=-1, pattern=[[1, P]],
                                                   channel_multiplier=-1).then_inc(b_const, 1)
                        pool.affine_select(out=neg_tri[:, :], in_=neg_tri[:, :], compare_op=ALU.is_ge, fill=0.0,
                                           base=0, pattern=[[-1, P]], channel_multiplier=1).then_inc(b_const, 1)

                    @block.scalar
                    def _(act):
                        def copy_qk(p):
                            act.wait_ge(st.unit_used, UN * p + UN)
                            nc.scalar.activation(q_sb[:, :, :], Q[:, :].rearrange("p (j t) -> p j t", j=2),
                                                 ACT.Copy, scale=SCALE).then_inc(b_qk, 1)
                            nc.scalar.activation(k_sb[:, :, :], K_[:, :].rearrange("p (j t) -> p j t", j=2),
                                                 ACT.Copy).then_inc(b_qk, 1)

                        def softplus(p):
                            for j in range(2):
                                act.wait_ge(b_z, 2 * p + j + 1)
                                nc.scalar.activation(z_abs[:, j, :], Z[j][:, 0:PA], ACT.Abs).then_inc(b_abs, 1)
                            act.wait_ge(b_abs, 2 * p + 2)
                            nc.scalar.activation(z_exp[:, :, :], z_abs[:, :, :], ACT.Exp, scale=-1.0).then_inc(b_e, 1)
                            act.wait_ge(b_e, p + 1)
                            nc.scalar.activation(z_ln[:, :, :], z_exp[:, :, :], ACT.Ln, bias=1.0).then_inc(b_ln, 1)

                        def weights(p):
                            act.wait_ge(b_expo, 2 * p + 2)
                            nc.scalar.activation(a_sb[:, :, :], expo[:, :, :], ACT.Exp).then_inc(b_a, 1)

                        def o_hi(p):
                            act.wait_ge(b_o, p + 1)
                            nc.scalar.activation(yT_hi[:, ds(KD + 2 * p, 2), :],
                                                 O_[:, :].rearrange("p (j t) -> p j t", j=2),
                                                 ACT.Copy).then_inc(b_ohi, 1)

                        def body(it, p):
                            for u in range(UN):
                                if it is not None:
                                    st.split_hi(act, it, u, isinstance(it, int) and it == 0, 2 * W)
                                if p is None:
                                    continue
                                if u == 0:
                                    copy_qk(p)
                                if u == 2:
                                    softplus(p)
                                if u == 5:
                                    weights(p)
                                if u == 7:
                                    o_hi(p)
                        body(0, None)
                        with act.Fori(1, N_IT) as it:
                            body(it, it - 1)
                        body(None, N_IT - 1)

                    @block.vector
                    def _(dve):
                        def copy_v(p):
                            dve.wait_ge(st.unit_used, UN * p + UN)
                            nc.vector.tensor_copy(v_sb[:, :, :], V[:, :].rearrange("p (s d) -> p s d", s=TB)).then_inc(b_v, 1)

                        def softplus(p):
                            dve.wait_ge(b_ln, p + 1)
                            for j in range(2):
                                nc.vector.scalar_tensor_tensor(out=splus[:, j, :], in0=Z[j][:, 0:PA], scalar=0.0,
                                                               in1=z_ln[:, j, :], op0=ALU.max,
                                                               op1=ALU.add).then_inc(b_sp1, 1)
                            for j in range(2):
                                dve.wait_ge(b_sp1, 2 * p + j + 1)
                                nc.vector.tensor_tensor(splus[:, j, :], splus[:, j, :], mask[:, :],
                                                        ALU.mult).then_inc(b_sp, 1)

                        def exponent(p):
                            for j in range(2):
                                dve.wait_ge(b_cum, 2 * p + j + 1)
                                nc.vector.scalar_tensor_tensor(out=expo[:, j, :], in0=Z[j][:, 0:PA], scalar=0.0,
                                                               in1=mask_neg[:, :], op0=ALU.min,
                                                               op1=ALU.add).then_inc(b_expo, 1)

                        def o_lo(p):
                            dve.wait_ge(b_ohi, p + 1)
                            here = ds(KD + 2 * p, 2)
                            nc.vector.tensor_tensor(yT_lo[:, here, :], O_[:, :].rearrange("p (j t) -> p j t", j=2),
                                                    yT_hi[:, here, :].bitcast(F32), ALU.subtract).then_inc(b_olo, 1)

                        def body(it, p):
                            for u in range(UN):
                                if it is not None:
                                    st.split_lo(dve, it, u, 2 * W)
                                if p is None:
                                    continue
                                if u == 0:
                                    copy_v(p)
                                if u == 2:
                                    softplus(p)
                                if u == 5:
                                    exponent(p)
                                if u == 7:
                                    o_lo(p)
                        dve.wait_ge(b_const, 9)
                        body(0, None)
                        with dve.Fori(1, N_IT) as it:
                            body(it, it - 1)
                        body(None, N_IT - 1)

                    @block.tensor
                    def _(pe):
                        mm = lambda out, l, r, start: nc.tensor.matmul(out, l, r, start=start, stop=True,
                                                                       skip_group_check=True)

                        def z(p):
                            pe.wait_ge(b_qk, 2 * p + 2)
                            for j in range(2):
                                if not (isinstance(p, int) and p == 0):
                                    pe.wait_ge(b_expo, 2 * p + j - 1)
                                mm(Z[j][:, 0:T], k_sb[:, j, 0:P], q_sb[:, j, :], True)
                                mm(Z[j][:, T:PA], k_sb[:, j, P:T], q_sb[:, j, P:T], False).then_inc(b_z, 1)

                        def cumulate(p):
                            for j in range(2):
                                pe.wait_ge(b_sp, 2 * p + j + 1)
                                mm(Z[j][:, 0:T], neg_tri[:, :], splus[:, j, 0:T], False)
                                mm(Z[j][:, T:PA], neg_tri[:, :], splus[:, j, T:PA], False)
                                mm(Z[j][:, P:T], neg_one[:, :], splus[:, j, T:PA], False).then_inc(b_cum, 1)

                        def outputs(p):
                            pe.wait_ge(b_a, p + 1)
                            if not (isinstance(p, int) and p == 0):
                                pe.wait_ge(b_olo, p)
                            for j in range(2):
                                d = slice(j * P, (j + 1) * P)
                                mm(O_[:, j * T:(j + 1) * T], v_sb[:, 0, d], a_sb[:, j, 0:T], j == 0)
                                last = mm(O_[:, j * T + P:(j + 1) * T], v_sb[:, 1, d], a_sb[:, j, T:PA], False)
                            last.then_inc(b_o, 1)

                        def body(it, p):
                            if p is not None and it is not None:
                                pe.wait_ge(b_qk, 2 * it)
                                pe.wait_ge(b_v, it)
                            for u in range(UN):
                                if it is not None:
                                    st.wait_unit(pe, it, u)
                                    for kk in range(2):
                                        k = 2 * u + kk
                                        xs = (xT_hi[:, k, :], xT_lo[:, k, :])
                                        for m in range(4):
                                            at = slice(kk * W + m * P, kk * W + (m + 1) * P)
                                            tri_matmul(bank[m // 2][:, (m % 2) * T:(m % 2 + 1) * T],
                                                       (st.hi[u % 2][:, at], st.lo[u % 2][:, at]), xs,
                                                       start=k == 0 and m % 2 == 0, stop=k == KD - 1)
                                        at = slice(kk * W + 512, kk * W + W)
                                        for tb in range(TB):
                                            t = slice(tb * P, (tb + 1) * P)
                                            last = tri_matmul(V[:, tb * T:(tb + 1) * T],
                                                              (xT_hi[:, k, t], xT_lo[:, k, t]),
                                                              (st.hi[u % 2][:, at], st.lo[u % 2][:, at]),
                                                              start=k == 0 and tb == 0, stop=k == KD - 1)
                                    last.then_inc(st.unit_used, 1)
                                if p is None:
                                    continue
                                if u == 1:
                                    z(p)
                                if u == 4:
                                    cumulate(p)
                                if u == 6:
                                    outputs(p)
                        pe.wait_ge(b_const, 9)
                        body(0, None)
                        body(1, 0)
                        with pe.Fori(2, N_IT) as it:
                            body(it, it - 1)
                        body(None, N_IT - 1)
            branch("gb", COL_G + D, w_branch_b, KD, KD)

            ssd = ExitStack()
            with ssd:
                upper = sb(ssd, "upper", [P, P])
                neg_upper = sb(ssd, "neg_upper", [P, P])
                ones = sb(ssd, "ones", [P, P])
                dt = sb(ssd, "dt", [P, TB, SSD_HEADS])
                da = sb(ssd, "da", [P, TB, SSD_HEADS])
                decay = sb(ssd, "decay", [P, SSD_HEADS])
                d_col = sb(ssd, "d_col", [P, KC])

                c = ExitStack()
                with c:
                    n_dt = KD * SSD_HEADS
                    w_raw = sb(c, "dt_w_raw", [P, n_dt])
                    w_hi = sb(c, "dt_w_hi", [P, n_dt], F32R)
                    w_lo = sb(c, "dt_w_lo", [P, n_dt], F32R)
                    bias = sb(c, "dt_bias", [P, SSD_HEADS])
                    a_log = sb(c, "dt_a_log", [P, SSD_HEADS])
                    a_neg = sb(c, "dt_a_exp", [P, SSD_HEADS])
                    below = sb(c, "dt_below", [P, P])
                    u = sb(c, "dt_u", [P, TB, SSD_HEADS])
                    u_abs = sb(c, "dt_u_abs", [P, TB, SSD_HEADS])
                    u_exp = sb(c, "dt_u_exp", [P, TB, SSD_HEADS])
                    u_ln = sb(c, "dt_u_ln", [P, TB, SSD_HEADS])
                    d_w = sem("d_w")
                    d_vec = sem("d_vec")
                    d_const = sem("d_const")
                    d_hi = sem("d_hi")
                    d_lo = sem("d_lo")
                    d_proj = sem("d_proj")
                    d_u = sem("d_u")
                    d_act = sem("d_act")
                    d_dt = sem("d_dt")
                    d_da = sem("d_da")
                    d_dec = sem("d_dec")
                    d_out = sem("d_out")
                    with nc.Block() as block:
                        @block.sync
                        def _(sp):
                            sp.dma_start(w_raw[:, :].rearrange("p (k n) -> p k n", k=KD),
                                         w_in[0, :, COL_DT:COL_DT + SSD_HEADS].rearrange(
                                             "(k p) n -> p k n", p=P)).then_inc(d_w, 16)
                            sp.dma_start(bias[:, :], ssd_dt_bias[0:1, :].to_broadcast([P, SSD_HEADS])).then_inc(d_vec, 16)
                            sp.dma_start(a_log[:, :], ssd_a_log[0:1, :].to_broadcast([P, SSD_HEADS])).then_inc(d_vec, 16)
                            heads = ssd_d.rearrange("o (c h) -> h (o c)", h=2)
                            for h in range(2):
                                sp.dma_start(d_col[64 * h:64 * h + 64, :],
                                             heads[h:h + 1, :].to_broadcast([64, KC]),
                                             allow_slow_non_contiguous=True).then_inc(d_vec, 16)

                        @block.gpsimd
                        def _(pool):
                            pool.memset(ones[:, :], 1.0).then_inc(d_const, 1)
                            pool.memset(upper[:, :], 1.0).then_inc(d_const, 1)
                            pool.memset(neg_upper[:, :], -1.0).then_inc(d_const, 1)
                            pool.memset(below[:, :], 1.0).then_inc(d_const, 1)
                            pool.wait_ge(d_const, 4)
                            for m in (upper, neg_upper):
                                pool.affine_select(out=m[:, :], in_=m[:, :], compare_op=ALU.is_ge, fill=0.0, base=0,
                                                   pattern=[[1, P]], channel_multiplier=-1).then_inc(d_const, 1)
                            pool.affine_select(out=below[:, :], in_=below[:, :], compare_op=ALU.is_ge, fill=0.0,
                                               base=-1, pattern=[[-1, P]], channel_multiplier=1).then_inc(d_const, 1)

                        @block.scalar
                        def _(act):
                            act.wait_ge(d_w, 16)
                            nc.scalar.activation(w_hi[:, :], w_raw[:, :], ACT.Copy).then_inc(d_hi, 1)
                            act.wait_ge(d_vec, 64)
                            nc.scalar.activation(a_neg[:, :], a_log[:, :], ACT.Exp).then_inc(d_act, 1)
                            act.wait_ge(d_u, 1)
                            nc.scalar.activation(u_abs[:, :, :], u[:, :, :], ACT.Abs).then_inc(d_act, 1)
                            act.wait_ge(d_act, 2)
                            nc.scalar.activation(u_exp[:, :, :], u_abs[:, :, :], ACT.Exp, scale=-1.0).then_inc(d_act, 1)
                            act.wait_ge(d_act, 3)
                            nc.scalar.activation(u_ln[:, :, :], u_exp[:, :, :], ACT.Ln, bias=1.0).then_inc(d_act, 1)
                            act.wait_ge(d_dec, 1)
                            nc.scalar.activation(decay[:, :], bank[1][:, 0:SSD_HEADS], ACT.Exp).then_inc(d_out, 1)

                        @block.vector
                        def _(dve):
                            dve.wait_ge(d_hi, 1)
                            nc.vector.tensor_tensor(w_lo[:, :], w_raw[:, :], w_hi[:, :].bitcast(F32),
                                                    ALU.subtract).then_inc(d_lo, 1)
                            dve.wait_ge(d_vec, 64)
                            dve.wait_ge(d_proj, 1)
                            for tb in range(TB):
                                last = nc.vector.tensor_tensor(u[:, tb, :],
                                                               bank[0][:, tb * SSD_HEADS:(tb + 1) * SSD_HEADS],
                                                               bias[:, :], ALU.add)
                            last.then_inc(d_u, 1)
                            dve.wait_ge(d_act, 4)
                            nc.vector.scalar_tensor_tensor(out=dt[:, :, :], in0=u[:, :, :], scalar=0.0,
                                                           in1=u_ln[:, :, :], op0=ALU.max, op1=ALU.add).then_inc(d_dt, 1)
                            dve.wait_ge(d_dt, 1)
                            for tb in range(TB):
                                last = nc.vector.scalar_tensor_tensor(out=da[:, tb, :], in0=dt[:, tb, :], scalar=-1.0,
                                                                      in1=a_neg[:, :], op0=ALU.mult, op1=ALU.mult)
                            last.then_inc(d_da, 1)

                        @block.tensor
                        def _(pe):
                            pe.wait_ge(d_lo, 1)
                            for k in range(KD):
                                at = slice(k * SSD_HEADS, (k + 1) * SSD_HEADS)
                                for tb in range(TB):
                                    t = slice(tb * P, (tb + 1) * P)
                                    last = tri_matmul(bank[0][:, tb * SSD_HEADS:(tb + 1) * SSD_HEADS],
                                                      (xT_hi[:, k, t], xT_lo[:, k, t]), (w_hi[:, at], w_lo[:, at]),
                                                      start=k == 0 and tb == 0, stop=k == KD - 1)
                            last.then_inc(d_proj, 1)
                            pe.wait_ge(d_const, 7)
                            pe.wait_ge(d_da, 1)
                            nc.tensor.matmul(bank[1][:, 0:SSD_HEADS], below[:, :], da[:, 0, :],
                                             start=True, stop=True).then_inc(d_dec, 1)

                c = ExitStack()
                with c:
                    W, UN, N_IT = 1280, 16, GROUPS
                    st = Stream(c, "c", W, UN, 4)
                    zs = sb(c, "c_zs", [P, 4, T])
                    xpad = sb(c, "c_xpad", [P, 6, T + 3])
                    xc = sb(c, "c_xc", [P, 6, T])
                    b_tok = sb(c, "c_b_tok", [P, P])
                    cbm = sb(c, "c_cbm", [P, TB, P])
                    xdt = sb(c, "c_xdt", [P, TB, 512])
                    xdd = sb(c, "c_xdd", [P, 512])
                    dag = sb(c, "c_dag", [P, TB, HPG])
                    wts = sb(c, "c_wts", [P, TB, HPG, P])
                    ce = sb(c, "c_ce", [P, HPG, P])
                    sq = ce[:, :, :].rearrange("p a b -> p (a b)").rearrange("p (a b) -> p a b", a=4)
                    prev = sb(c, "c_prev", [P, 512])
                    yz = sb(c, "c_yz", [P, 4, T])
                    rs_ln = sb(c, "c_rs_ln", [P, T])
                    rs = sb(c, "c_rs", [P, T])
                    s = {n: sem("c_" + n) for n in (
                        "pad", "evac", "conv", "xc", "tr", "btok", "cbm", "xdt", "dag", "diff", "min", "exp", "wts",
                        "cs", "ecs", "prev", "ce", "y", "skip", "yz", "sq", "sum", "rsl", "rs", "yn", "yhi", "ylo")}
                    first_p = lambda p: isinstance(p, int) and p == 0
                    with nc.Block() as block:
                        @block.sync
                        def _(sp):
                            def body(it, first):
                                for u in range(UN):
                                    raw = st.raw[u % 4]
                                    r = slice(u * P, (u + 1) * P)
                                    st.load(sp, it, u, first, [
                                        (raw[:, 512:1024], w_in[0, r, ds(COL_XS + it * 512, 512)]),
                                        (raw[:, 0:512], w_in[0, r, ds(COL_Z + it * 512, 512)]),
                                        (raw[:, 1024:1152], w_in[0, r, ds(COL_BM + it * P, P)]),
                                        (raw[:, 1152:1280], w_in[0, r, ds(COL_CM + it * P, P)])])
                            body(0, True)
                            with sp.Fori(1, N_IT) as it:
                                body(it, False)

                        @block.gpsimd
                        def _(pool):
                            pool.memset(xpad[:, :, :], 0.0).then_inc(s["pad"], 1)

                            def scale_c(p):
                                pool.wait_ge(s["ecs"], 2 * p + 2)
                                pool.tensor_tensor(ce[:, :, :], ce[:, :, :],
                                                   xc[:, 5:6, P:T].to_broadcast([P, HPG, P]),
                                                   ALU.mult).then_inc(s["ce"], 1)
                            scale_c(0)
                            with pool.Fori(1, N_IT) as p:
                                scale_c(p)

                        @block.scalar
                        def _(act):
                            def evacuate(p):
                                act.wait_ge(st.unit_used, UN * p + UN)
                                if first_p(p):
                                    act.wait_ge(s["pad"], 1)
                                for i in range(3):
                                    nc.scalar.activation(xpad[:, 2 * i:2 * i + 2, 3:T + 3],
                                                         bank[2 + i][:, :].rearrange("p (j t) -> p j t", j=2),
                                                         ACT.Copy).then_inc(s["evac"], 1)
                                for i in range(2):
                                    nc.scalar.activation(zs[:, 2 * i:2 * i + 2, :],
                                                         bank[i][:, :].rearrange("p (j t) -> p j t", j=2),
                                                         ACT.Silu).then_inc(s["evac"], 1)

                            def silu_x(p):
                                act.wait_ge(s["conv"], 24 * p + 24)
                                nc.scalar.activation(xc[:, :, :], xc[:, :, :], ACT.Silu).then_inc(s["xc"], 1)

                            def b_tokens(p):
                                act.wait_ge(s["tr"], 3 * p + 3)
                                nc.scalar.activation(b_tok[:, :], bank[7][:, 0:P], ACT.Copy).then_inc(s["btok"], 1)

                            def exp_w(p, ch):
                                for q in range(2):
                                    act.wait_ge(s["min"], 4 * p + 2 * ch + q + 1)
                                    here = wts[:, ch, 4 * q:4 * q + 4, :]
                                    nc.scalar.activation(here, here, ACT.Exp).then_inc(s["exp"], 1)

                            def exp_cs(p):
                                for q in range(2):
                                    act.wait_ge(s["cs"], 3 * p + q + 1)
                                    nc.scalar.activation(ce[:, 4 * q:4 * q + 4, :],
                                                         bank[5 + q][:, :].rearrange("p (h l) -> p h l", h=4),
                                                         ACT.Exp).then_inc(s["ecs"], 1)
                                act.wait_ge(s["cs"], 3 * p + 3)
                                nc.scalar.activation(prev[:, :], bank[7][:, :], ACT.Copy).then_inc(s["prev"], 1)

                            def square(p):
                                act.wait_ge(s["yz"], p + 1)
                                nc.scalar.activation(sq, yz[:, :, :], ACT.Square).then_inc(s["sq"], 1)

                            def inv_rms(r):
                                act.wait_ge(s["sum"], r + 1)
                                nc.scalar.activation(rs_ln[:, :], bank[7][:, 0:T], ACT.Ln, bias=eps_col[:, 0:1],
                                                     scale=1.0 / 512).then_inc(s["rsl"], 1)
                                act.wait_ge(s["rsl"], r + 1)
                                nc.scalar.activation(rs[:, :], rs_ln[:, :], ACT.Exp, scale=-0.5).then_inc(s["rs"], 1)

                            def y_hi(r):
                                act.wait_ge(s["yn"], 4 * r + 4)
                                nc.scalar.activation(yT_hi[:, ds(4 * r, 4), :], yz[:, :, :], ACT.Copy).then_inc(s["yhi"], 1)

                            def body(it, p, r):
                                for u in range(UN):
                                    if it is not None:
                                        st.split_hi(act, it, u, first_p(it), W)
                                    if p is not None:
                                        if u == 0:
                                            evacuate(p)
                                        if u == 4:
                                            silu_x(p)
                                        if u == 7:
                                            b_tokens(p)
                                        if u == 10:
                                            exp_w(p, 0)
                                        if u == 12:
                                            exp_w(p, 1)
                                        if u == 13:
                                            exp_cs(p)
                                        if u == 15:
                                            square(p)
                                    if r is not None:
                                        if u == 1:
                                            inv_rms(r)
                                        if u == 4:
                                            y_hi(r)
                            body(0, None, None)
                            body(1, 0, None)
                            with act.Fori(2, N_IT) as it:
                                body(it, it - 1, it - 2)
                            body(None, N_IT - 1, N_IT - 2)
                            body(None, None, N_IT - 1)

                        @block.vector
                        def _(dve):
                            def conv(p, i):
                                dve.wait_ge(s["evac"], 5 * p + i + 1)
                                for b in (2 * i, 2 * i + 1):
                                    ch = 4 * p + b if b < 4 else (32 + p if b == 4 else 40 + p)
                                    w = lambda k: vcols[:, ds(V_SSDW + 48 * k + ch, 1)]
                                    nc.vector.tensor_scalar(xc[:, b, :], xpad[:, b, 3:T + 3], w(3),
                                                            vcols[:, ds(V_CONVB + ch, 1)], ALU.mult,
                                                            ALU.add).then_inc(s["conv"], 1)
                                    for k in (2, 1, 0):
                                        dve.wait_ge(s["conv"], 24 * p + 4 * b + 3 - k)
                                        nc.vector.scalar_tensor_tensor(
                                            out=xc[:, b, :], in0=xpad[:, b, k:k + T], scalar=w(k), in1=xc[:, b, :],
                                            op0=ALU.mult, op1=ALU.add).then_inc(s["conv"], 1)

                            def per_head(a):
                                return a.unsqueeze(2).to_broadcast([P, HPG, 64])

                            def tokens(p):
                                here = ds(HPG * p, HPG)
                                nc.vector.tensor_copy(dag[:, :, :], da[:, :, here]).then_inc(s["dag"], 1)
                                for tb in range(TB):
                                    dve.wait_ge(s["tr"], 3 * p + tb + 1)
                                    nc.vector.tensor_tensor(xdt[:, tb, :].rearrange("p (h d) -> p h d", h=HPG),
                                                            bank[5 + tb][:, :].rearrange("p (h d) -> p h d", h=HPG),
                                                            per_head(dt[:, tb, here]), ALU.mult).then_inc(s["xdt"], 1)
                                dve.wait_ge(s["xdt"], 2 * p + 1)
                                nc.vector.tensor_tensor(xdd[:, :].rearrange("p (h d) -> p h d", h=HPG),
                                                        xdt[:, 0, :].rearrange("p (h d) -> p h d", h=HPG),
                                                        per_head(decay[:, here]), ALU.mult)
                                dve.wait_ge(s["btok"], p + 1)
                                for ch in range(TB):
                                    nc.vector.tensor_tensor(cbm[:, ch, :], bank[7][:, P + ch * P:2 * P + ch * P],
                                                            upper[:, :], ALU.mult).then_inc(s["cbm"], 1)

                            def clamp(p, ch):
                                for q in range(2):
                                    dve.wait_ge(s["diff"], 4 * p + 2 * ch + q + 1)
                                    nc.vector.tensor_scalar(wts[:, ch, 4 * q:4 * q + 4, :],
                                                            bank[5 + q][:, :].rearrange("p (h l) -> p h l", h=4),
                                                            0.0, None, ALU.min).then_inc(s["min"], 1)

                            def weights(p, ch):
                                for q in range(2):
                                    dve.wait_ge(s["exp"], 4 * p + 2 * ch + q + 1)
                                    here = wts[:, ch, 4 * q:4 * q + 4, :]
                                    nc.vector.tensor_tensor(here, here, cbm[:, ch:ch + 1, :].to_broadcast([P, 4, P]),
                                                            ALU.mult).then_inc(s["wts"], 1)

                            def skip_gate(p):
                                for j in range(4):
                                    dve.wait_ge(s["y"], 2 * p + j // 2 + 1)
                                    nc.vector.scalar_tensor_tensor(
                                        out=yz[:, j, :], in0=xc[:, j, :], scalar=d_col[:, ds(4 * p + j, 1)],
                                        in1=bank[5 + j // 2][:, (j % 2) * T:(j % 2 + 1) * T],
                                        op0=ALU.mult, op1=ALU.add).then_inc(s["skip"], 1)
                                dve.wait_ge(s["skip"], 4 * p + 4)
                                nc.vector.tensor_tensor(yz[:, :, :], yz[:, :, :], zs[:, :, :], ALU.mult).then_inc(s["yz"], 1)

                            def normalise(r):
                                dve.wait_ge(s["rs"], r + 1)
                                for j in range(4):
                                    nc.vector.scalar_tensor_tensor(
                                        out=yz[:, j, :], in0=yz[:, j, :], scalar=vcols[:, ds(V_SSDN + 4 * r + j, 1)],
                                        in1=rs[:, :], op0=ALU.mult, op1=ALU.mult).then_inc(s["yn"], 1)

                            def y_lo(r):
                                dve.wait_ge(s["yhi"], r + 1)
                                here = ds(4 * r, 4)
                                nc.vector.tensor_tensor(yT_lo[:, here, :], yz[:, :, :], yT_hi[:, here, :].bitcast(F32),
                                                        ALU.subtract).then_inc(s["ylo"], 1)

                            def body(it, p, r):
                                for u in range(UN):
                                    if it is not None:
                                        st.split_lo(dve, it, u, W)
                                    if p is not None and u < 3:
                                        conv(p, u)
                                    if r is not None:
                                        if u == 3:
                                            normalise(r)
                                        if u == 5:
                                            y_lo(r)
                                    if p is not None:
                                        if u == 7:
                                            tokens(p)
                                        if u == 9:
                                            clamp(p, 0)
                                        if u == 11:
                                            clamp(p, 1)
                                            weights(p, 0)
                                        if u == 13:
                                            weights(p, 1)
                                        if u == 15:
                                            skip_gate(p)
                            body(0, None, None)
                            body(1, 0, None)
                            with dve.Fori(2, N_IT) as it:
                                body(it, it - 1, it - 2)
                            body(None, N_IT - 1, N_IT - 2)
                            body(None, None, N_IT - 1)

                        @block.tensor
                        def _(pe):
                            mm = lambda out, l, r, start: nc.tensor.matmul(out, l, r, start=start, stop=True,
                                                                           skip_group_check=True)

                            def turn(p):
                                pe.wait_ge(s["xc"], p + 1)
                                if not first_p(p):
                                    pe.wait_ge(s["yz"], p)
                                    pe.wait_ge(s["rsl"], p)
                                for tb in range(TB):
                                    t = slice(tb * P, (tb + 1) * P)
                                    for j in range(4):
                                        last = nc.tensor.transpose(bank[5 + tb][:, j * P:(j + 1) * P],
                                                                   xc[:, j, t], ident[:, :])
                                    last.then_inc(s["tr"], 1)
                                nc.tensor.transpose(bank[7][:, 0:P], xc[:, 4, 0:P], ident[:, :])
                                for ch in range(TB):
                                    t = slice(ch * P, (ch + 1) * P)
                                    last = mm(bank[7][:, P + ch * P:2 * P + ch * P], xc[:, 4, t], xc[:, 5, t], True)
                                last.then_inc(s["tr"], 1)

                            def bcast(ch, h):
                                return dag[:, ch, h:h + 1].to_broadcast([P, P])

                            def diffs(p, ch):
                                if ch == 0:
                                    pe.wait_ge(s["dag"], p + 1)
                                    pe.wait_ge(s["xdt"], 2 * p + 2)
                                else:
                                    pe.wait_ge(s["min"], 4 * p + 2)
                                for q in range(2):
                                    for h in range(4):
                                        mm(bank[5 + q][:, h * P:(h + 1) * P], bcast(ch, 4 * q + h), upper[:, :], h == 0)
                                    mm(bank[5 + q][:, :].rearrange("p (h l) -> p h l", h=4), neg_upper[:, :],
                                       dag[:, ch, 4 * q:4 * q + 4].unsqueeze(2).to_broadcast([P, 4, P]),
                                       False).then_inc(s["diff"], 1)

                            def sums_states(p):
                                pe.wait_ge(s["min"], 4 * p + 4)
                                for q in range(2):
                                    for h in range(4):
                                        last = mm(bank[5 + q][:, h * P:(h + 1) * P], bcast(1, 4 * q + h), upper[:, :], h == 0)
                                    last.then_inc(s["cs"], 1)
                                pe.wait_ge(s["cbm"], 2 * p + 2)
                                mm(bank[7][:, :], b_tok[:, :], xdd[:, :], True).then_inc(s["cs"], 1)

                            def outputs(p):
                                pe.wait_ge(s["wts"], 4 * p + 4)
                                pe.wait_ge(s["ce"], p + 1)
                                pe.wait_ge(s["prev"], p + 1)
                                for i in range(2):
                                    for j in (2 * i, 2 * i + 1):
                                        for hh in range(2):
                                            h = 2 * j + hh
                                            rows = slice(64 * hh, 64 * hh + 64)
                                            o = lambda ch: bank[5 + i][rows, (j % 2) * T + ch * P:(j % 2) * T + ch * P + P]
                                            x_of = slice(64 * h, 64 * h + 64)
                                            mm(o(0), xdt[:, 0, x_of], wts[:, 0, h, :], True)
                                            mm(o(1), xdt[:, 1, x_of], wts[:, 1, h, :], True)
                                            last = mm(o(1), prev[:, x_of], ce[:, h, :], False)
                                    last.then_inc(s["y"], 1)

                            def square_sum(p):
                                pe.wait_ge(s["sq"], p + 1)
                                for j in range(4):
                                    last = mm(bank[7][:, 0:T], ones[:, :], sq[:, j, :], j == 0)
                                last.then_inc(s["sum"], 1)

                            def body(it, p):
                                if it is not None and p is not None:
                                    pe.wait_ge(s["evac"], 5 * it)
                                for u in range(UN):
                                    if it is not None:
                                        st.wait_unit(pe, it, u)
                                        xs = (xT_hi[:, u, :], xT_lo[:, u, :])
                                        for m in range(10):
                                            at = slice(m * P, (m + 1) * P)
                                            last = tri_matmul(bank[m // 2][:, (m % 2) * T:(m % 2 + 1) * T],
                                                              (st.hi[u % 2][:, at], st.lo[u % 2][:, at]), xs,
                                                              start=u == 0 and m % 2 == 0, stop=u == KD - 1)
                                        last.then_inc(st.unit_used, 1)
                                    if p is None:
                                        continue
                                    if u == 5:
                                        turn(p)
                                    if u == 7:
                                        diffs(p, 0)
                                    if u == 9:
                                        diffs(p, 1)
                                    if u == 11:
                                        sums_states(p)
                                    if u == 13:
                                        outputs(p)
                                    if u == 15:
                                        square_sum(p)
                            body(0, None)
                            body(1, 0)
                            with pe.Fori(2, N_IT) as it:
                                body(it, it - 1)
                            body(None, N_IT - 1)
            branch("gc", COL_G + 2 * D, w_branch_c, KC, 0)

            c = ExitStack()
            with c:
                UN, N_IT = 4, D // 512
                st = Stream(c, "o", 4 * 512, UN, 2)
                o_tr = sem("o_tr")
                o_hi = sem("o_hi")
                o_lo = sem("o_lo")
                o_x = sem("o_x")
                o_h = sem("o_h")
                with nc.Block() as block:
                    @block.sync
                    def _(sp):
                        def body(it, first):
                            for u in range(UN):
                                raw = st.raw[u][:, :].rearrange("p (k n) -> p k n", k=4)
                                st.load(sp, it, u, first, [
                                    (raw[:, half * 2:half * 2 + 2, :],
                                     w_out[0, u * 512 + half * 256:u * 512 + half * 256 + 256,
                                           ds(it * 512, 512)].rearrange("(k p) n -> p k n", p=P)) for half in (1, 0)])
                        body(0, True)
                        sp.wait_ge(o_tr, KD)
                        for tb in range(TB):
                            sp.dma_start(acc[:, tb, :], x[0, tb * P:(tb + 1) * P, :]).then_inc(o_x, 16)
                        with sp.Fori(1, N_IT) as it:
                            body(it, False)

                    @block.scalar
                    def _(act):
                        for k in range(KD):
                            act.wait_ge(o_tr, 2 * (k // 2) + 2)
                            nc.scalar.activation(yT_hi[:, k, :], bank[2 + (k // 2) % 4][:, (k % 2) * T:(k % 2 + 1) * T],
                                                 ACT.Copy).then_inc(o_hi, 1)

                        def body(it, first):
                            for u in range(UN):
                                st.split_hi(act, it, u, first, 2048)
                        body(0, True)
                        with act.Fori(1, N_IT) as it:
                            body(it, False)

                    @block.vector
                    def _(dve):
                        for k in range(KD):
                            dve.wait_ge(o_hi, 2 * (k // 2) + 2)
                            nc.vector.tensor_tensor(yT_lo[:, k, :], bank[2 + (k // 2) % 4][:, (k % 2) * T:(k % 2 + 1) * T],
                                                    yT_hi[:, k, :].bitcast(F32), ALU.subtract).then_inc(o_lo, 1)

                        def residual(p):
                            dve.wait_ge(st.unit_used, UN * p + UN)
                            if isinstance(p, int):
                                dve.wait_ge(o_x, 16 * TB)
                            for tb in range(TB):
                                here = acc[:, tb, ds(p * 512, 512)]
                                nc.vector.tensor_tensor(here, here, bank[tb][:, :], ALU.add).then_inc(o_h, 1)

                        def body(it, p):
                            for u in range(UN):
                                st.split_lo(dve, it, u, 2048)
                                if p is not None and u == 0:
                                    residual(p)
                        body(0, None)
                        body(1, 0)
                        with dve.Fori(2, N_IT) as it:
                            body(it, it - 1)
                        residual(N_IT - 1)

                    @block.tensor
                    def _(pe):
                        for k in range(KD):
                            if k >= 8:
                                pe.wait_ge(o_lo, 2 * (k // 2 - 4) + 2)
                            for tb in range(TB):
                                at = (k % 2) * T + tb * P
                                last = nc.tensor.transpose(bank[2 + (k // 2) % 4][:, at:at + P],
                                                           acc[:, tb, k * P:(k + 1) * P], ident[:, :])
                            last.then_inc(o_tr, 1)
                        pe.wait_ge(o_lo, KD)

                        def body(it, first):
                            if not first:
                                pe.wait_ge(o_h, TB * it)
                            for u in range(UN):
                                st.wait_unit(pe, it, u)
                                for kk in range(4):
                                    k = 4 * u + kk
                                    at = slice(kk * 512, (kk + 1) * 512)
                                    for tb in range(TB):
                                        t = slice(tb * P, (tb + 1) * P)
                                        last = tri_matmul(bank[tb][:, :], (yT_hi[:, k, t], yT_lo[:, k, t]),
                                                          (st.hi[u % 2][:, at], st.lo[u % 2][:, at]),
                                                          start=k == 0, stop=k == KD - 1)
                                last.then_inc(st.unit_used, 1)
                        body(0, True)
                        with pe.Fori(1, N_IT) as it:
                            body(it, False)

        nc.clear_and_free_semaphores([h.num for h in live])
        nc.all_engine_barrier()
        live.clear()

        peer = ExitStack()
        with peer:
            n2 = sb(peer, "n2", [P, TB, D])
            gates = sb(peer, "gates", [P, TB, PH * PK])
            experts = sb(peer, "experts", [P, TB, PH * PK], U32)
            rte = ExitStack()
            with rte:
                nT_hi = sb(rte, "nT_hi", [P, KD, T], F32R)
                nT_lo = sb(rte, "nT_lo", [P, KD, T], F32R)
                keysT = sb(rte, "keysT", [P, 2 * PH, PN])
                c = ExitStack()
                with c:
                    wide = sb(c, "f_wide", [P, D])
                    keys = sb(c, "f_keys", [P, 2 * PH, P])
                    junk = sb(c, "f_junk", [P, D])
                    ssq = sb(c, "f_ssq", [P, TB])
                    std = sb(c, "f_std", [P, TB])
                    rstd = sb(c, "f_rstd", [P, TB])
                    f_in = sem("f_in")
                    f_ssq = sem("f_ssq")
                    f_std = sem("f_std")
                    f_rstd = sem("f_rstd")
                    f_scaled = sem("f_scaled")
                    f_xT = sem("f_xT")
                    f_hi = sem("f_hi")
                    f_lo = sem("f_lo")
                    f_keys = sem("f_keysT")
                    f_n = sem("f_n")
                    f_kc = sem("f_kc")
                    with nc.Block() as block:
                        @block.sync
                        def _(sp):
                            sp.dma_start(keys[:, :, :], peer_sub_keys[0].rearrange("h c n d -> n (h c) d")).then_inc(f_in, 16)
                            sp.dma_start(wide[:, :], norm_ffn_w[0:1, :].to_broadcast([P, D])).then_inc(f_in, 16)

                        @block.scalar
                        def _(act):
                            for tb in range(TB):
                                if tb:
                                    act.wait_ge(f_ssq, tb)
                                nc.scalar.activation(junk[:, :], acc[:, tb, :], ACT.Square,
                                                     accum_out=ssq[:, tb:tb + 1]).then_inc(f_ssq, 1)
                            act.wait_ge(f_ssq, TB)
                            nc.scalar.activation(std[:, :], ssq[:, :], ACT.Sqrt, bias=eps_col[:, 0:1],
                                                 scale=1.0 / D).then_inc(f_std, 1)
                            for k in range(KD):
                                act.wait_ge(f_xT, 2 * (k // 2) + 2)
                                nc.scalar.activation(nT_hi[:, k, :], bank[(k // 2) % 4][:, (k % 2) * T:(k % 2 + 1) * T],
                                                     ACT.Copy, scale=vcols[:, V_FFN + k:V_FFN + k + 1]).then_inc(f_hi, 1)
                            for b in range(4):
                                act.wait_ge(f_keys, b + 1)
                                nc.scalar.activation(keysT[:, 4 * b:4 * b + 4, :],
                                                     bank[4 + b][:, :].rearrange("p (k n) -> p k n", k=4),
                                                     ACT.Copy).then_inc(f_kc, 1)

                        @block.vector
                        def _(dve):
                            dve.wait_ge(f_std, 1)
                            nc.vector.reciprocal(rstd[:, :], std[:, :]).then_inc(f_rstd, 1)
                            dve.wait_ge(f_rstd, 1)
                            for tb in range(TB):
                                nc.vector.tensor_scalar(n2[:, tb, :], acc[:, tb, :], rstd[:, tb:tb + 1], None,
                                                        ALU.mult).then_inc(f_scaled, 1)
                            for k in range(KD):
                                dve.wait_ge(f_hi, 2 * (k // 2) + 2)
                                nc.vector.scalar_tensor_tensor(
                                    out=nT_lo[:, k, :], in0=bank[(k // 2) % 4][:, (k % 2) * T:(k % 2 + 1) * T],
                                    scalar=vcols[:, V_FFN + k:V_FFN + k + 1], in1=nT_hi[:, k, :].bitcast(F32),
                                    op0=ALU.mult, op1=ALU.subtract).then_inc(f_lo, 1)
                            dve.wait_ge(f_in, 32)
                            dve.wait_ge(f_xT, KD)
                            for tb in range(TB):
                                nc.vector.tensor_tensor(n2[:, tb, :], n2[:, tb, :], wide[:, :], ALU.mult).then_inc(f_n, 1)

                        @block.tensor
                        def _(pe):
                            pe.wait_ge(f_in, 32)
                            for b in range(4):
                                for j in range(4):
                                    last = nc.tensor.transpose(bank[4 + b][:, j * P:(j + 1) * P],
                                                               keys[:, 4 * b + j, :], ident[:, :])
                                last.then_inc(f_keys, 1)
                            pe.wait_ge(f_scaled, TB)
                            for k in range(KD):
                                if k >= 8:
                                    pe.wait_ge(f_lo, 2 * (k // 2 - 4) + 2)
                                for tb in range(TB):
                                    at = (k % 2) * T + tb * P
                                    last = nc.tensor.transpose(bank[(k // 2) % 4][:, at:at + P],
                                                               n2[:, tb, k * P:(k + 1) * P], ident[:, :])
                                last.then_inc(f_xT, 1)

                qT = sb(rte, "qT", [P, 2 * PH, T])
                scores = sb(rte, "scores", [P, TB, 2 * PH, PN])
                c = ExitStack()
                with c:
                    UN, N_IT = 4, D // 512
                    st = Stream(c, "q", 4 * 512, UN, 2)
                    q_c0 = sem("q_copied0")
                    q_c1 = sem("q_copied1")
                    q_s = sem("q_scores")
                    q_sc = sem("q_scores_copied")
                    with nc.Block() as block:
                        @block.sync
                        def _(sp):
                            def body(it, first):
                                for u in range(UN):
                                    raw = st.raw[u][:, :].rearrange("p (k n) -> p k n", k=4)
                                    st.load(sp, it, u, first, [
                                        (raw[:, half * 2:half * 2 + 2, :],
                                         peer_w_query[0, u * 512 + half * 256:u * 512 + half * 256 + 256,
                                                      ds(it * 512, 512)].rearrange("(k p) n -> p k n", p=P))
                                        for half in (1, 0)])
                            body(0, True)
                            with sp.Fori(1, N_IT) as it:
                                body(it, False)

                        @block.scalar
                        def _(act):
                            def copy(p):
                                act.wait_ge(st.unit_used, UN * p + UN)
                                nc.scalar.activation(qT[:, ds(4 * p, 2), :],
                                                     bank[0][:, :].rearrange("p (j t) -> p j t", j=2),
                                                     ACT.Copy).then_inc(q_c0, 1)

                            def body(it, p):
                                for u in range(UN):
                                    st.split_hi(act, it, u, p is None, 2048)
                                    if p is not None and u == 0:
                                        copy(p)
                            body(0, None)
                            with act.Fori(1, N_IT) as it:
                                body(it, it - 1)
                            copy(N_IT - 1)
                            for i in (0, 2, 4, 6):
                                act.wait_ge(q_s, i + 1)
                                nc.scalar.activation(scores[:, i // 4, 4 * (i % 4):4 * (i % 4) + 4, :],
                                                     bank[i][:, :].rearrange("p (k n) -> p k n", k=4),
                                                     ACT.Copy).then_inc(q_sc, 1)

                        @block.vector
                        def _(dve):
                            def copy(p):
                                dve.wait_ge(st.unit_used, UN * p + UN)
                                nc.vector.tensor_copy(qT[:, ds(4 * p + 2, 2), :],
                                                      bank[1][:, :].rearrange("p (j t) -> p j t", j=2)).then_inc(q_c1, 1)

                            def body(it, p):
                                for u in range(UN):
                                    st.split_lo(dve, it, u, 2048)
                                    if p is not None and u == 0:
                                        copy(p)
                            body(0, None)
                            with dve.Fori(1, N_IT) as it:
                                body(it, it - 1)
                            copy(N_IT - 1)
                            for i in (1, 3, 5, 7):
                                dve.wait_ge(q_s, i + 1)
                                nc.vector.tensor_copy(scores[:, i // 4, 4 * (i % 4):4 * (i % 4) + 4, :],
                                                      bank[i][:, :].rearrange("p (k n) -> p k n", k=4)).then_inc(q_sc, 1)

                        @block.tensor
                        def _(pe):
                            def body(it, first):
                                if not first:
                                    pe.wait_ge(q_c0, it)
                                    pe.wait_ge(q_c1, it)
                                for u in range(UN):
                                    st.wait_unit(pe, it, u)
                                    for kk in range(4):
                                        k = 4 * u + kk
                                        for m in range(4):
                                            at = slice(kk * 512 + m * P, kk * 512 + (m + 1) * P)
                                            last = tri_matmul(bank[m // 2][:, (m % 2) * T:(m % 2 + 1) * T],
                                                              (st.hi[u % 2][:, at], st.lo[u % 2][:, at]),
                                                              (nT_hi[:, k, :], nT_lo[:, k, :]),
                                                              start=k == 0 and m % 2 == 0, stop=k == KD - 1)
                                    last.then_inc(st.unit_used, 1)
                            body(0, True)
                            with pe.Fori(1, N_IT) as it:
                                body(it, False)
                            pe.wait_ge(q_c0, N_IT)
                            pe.wait_ge(q_c1, N_IT)
                            for i in range(8):
                                tb, g = i // 4, i % 4
                                for j in range(4):
                                    last = nc.tensor.matmul(bank[i][:, j * PN:(j + 1) * PN],
                                                            qT[:, 4 * g + j, tb * P:(tb + 1) * P], keysT[:, 4 * g + j, :],
                                                            start=True, stop=True)
                                last.then_inc(q_s, 1)

                c = ExitStack()
                with c:
                    R, KEYS = TB * PH, 2 * TB * PH
                    top_s = sb(c, "t_top_s", [P, KEYS, PK])
                    top_i = sb(c, "t_top_i", [P, KEYS, PK], U32)
                    key_f = sb(c, "t_key_f", [P, KEYS, PK])
                    left = sb(c, "t_left", [P, KEYS, PN])
                    cand = sb(c, "t_cand", [P, R, PK * PK])
                    cand2 = sb(c, "t_cand2", [P, R, PK * PK])
                    best = sb(c, "t_best", [P, R, PK])
                    pos = sb(c, "t_pos", [P, R, PK], U32)
                    side_u = sb(c, "t_side_u", [P, 2, R * PK], U32)
                    side_f = sb(c, "t_side_f", [P, 2, R * PK])
                    iota_u = sb(c, "t_iota_u", [P, PK], U32)
                    iota_f = sb(c, "t_iota_f", [P, PK])
                    key_of = sb(c, "t_key_of", [P, 2, R, PK])
                    idx_f = sb(c, "t_idx_f", [P, R * PK])
                    diff = sb(c, "t_diff", [P, R, PK])
                    expd = sb(c, "t_expd", [P, R, PK])
                    total = sb(c, "t_total", [P, R])
                    inv = sb(c, "t_inv", [P, R])
                    t_step = sem("t_step")
                    t_iota = sem("t_iota")
                    t_max = sem("t_max")
                    t_idx = sem("t_idx")
                    t_rep = sem("t_rep")
                    t_diff = sem("t_diff_done")
                    t_exp = sem("t_exp")
                    with nc.Block() as block:
                        @block.gpsimd
                        def _(pool):
                            pool.iota(iota_u[:, :], pattern=[[1, PK]], base=0, channel_multiplier=0).then_inc(t_iota, 1)

                        @block.scalar
                        def _(act):
                            act.wait_ge(t_diff, 1)
                            nc.scalar.activation(expd[:, :, :], diff[:, :, :], ACT.Exp).then_inc(t_exp, 1)

                        @block.vector
                        def _(dve):
                            v = nc.vector
                            flat = lambda a: a[:, :, :].rearrange("p a b -> p (a b)")

                            def sixteen(n, vals, rest, out_s, out_i, base):
                                for r in range(n):
                                    v.max(out_s[:, r, 0:8], vals(r)).then_inc(t_max, 1)
                                for r in range(n):
                                    dve.wait_ge(t_max, base[0] + r + 1)
                                    v.max_index(out_i[:, r, 0:8], out_s[:, r, 0:8], vals(r)).then_inc(t_idx, 1)
                                    v.match_replace(rest[:, r, :], out_s[:, r, 0:8], vals(r), -3.0e38).then_inc(t_rep, 1)
                                for r in range(n):
                                    dve.wait_ge(t_rep, base[1] + r + 1)
                                    v.max(out_s[:, r, 8:16], rest[:, r, :]).then_inc(t_max, 1)
                                for r in range(n):
                                    dve.wait_ge(t_max, base[0] + n + r + 1)
                                    v.max_index(out_i[:, r, 8:16], out_s[:, r, 8:16], rest[:, r, :]).then_inc(t_idx, 1)

                            sixteen(KEYS, lambda r: scores[:, r // (2 * PH), r % (2 * PH), :], left, top_s, top_i, (0, 0))
                            dve.wait_ge(t_idx, 2 * KEYS)
                            v.tensor_copy(flat(key_f), flat(top_i)).then_inc(t_step, 1)
                            sides = top_s[:, :, :].rearrange("p (r s) k -> p r s k", s=2)
                            for r in range(R):
                                v.tensor_tensor(cand[:, r, :].rearrange("p (a b) -> p a b", a=PK),
                                                sides[:, r, 0, :].unsqueeze(2).to_broadcast([P, PK, PK]),
                                                sides[:, r, 1, :].unsqueeze(1).to_broadcast([P, PK, PK]),
                                                ALU.add).then_inc(t_step, 1)
                            dve.wait_ge(t_step, 1 + R)
                            sixteen(R, lambda r: cand[:, r, :], cand2, best, pos, (2 * KEYS, KEYS))

                            v.tensor_tensor(diff[:, :, :], best[:, :, :], best[:, :, 0:1].to_broadcast([P, R, PK]),
                                            ALU.subtract).then_inc(t_diff, 1)
                            dve.wait_ge(t_idx, 2 * KEYS + 2 * R)
                            v.tensor_single_scalar(side_u[:, 0, :], flat(pos), 4, ALU.logical_shift_right).then_inc(t_step, 1)
                            v.tensor_single_scalar(side_u[:, 1, :], flat(pos), 15, ALU.bitwise_and).then_inc(t_step, 1)
                            dve.wait_ge(t_iota, 1)
                            v.tensor_copy(iota_f[:, :], iota_u[:, :]).then_inc(t_step, 1)
                            dve.wait_ge(t_step, R + 4)
                            v.tensor_copy(side_f[:, :, :], side_u[:, :, :]).then_inc(t_step, 1)
                            n = R + 5
                            keys_of = key_f[:, :, :].rearrange("p (r s) k -> p r s k", s=2)
                            for side in range(2):
                                hit = (cand, cand2)[side]
                                hit4 = hit[:, :, :].rearrange("p r (k a) -> p r k a", k=PK)
                                place = side_f[:, side, :].rearrange("p (r k) -> p r k", r=R)
                                dve.wait_ge(t_step, R + 5)
                                for r in range(R):
                                    v.tensor_tensor(hit4[:, r], place[:, r, :].unsqueeze(2).to_broadcast([P, PK, PK]),
                                                    iota_f[:, :].unsqueeze(1).to_broadcast([P, PK, PK]),
                                                    ALU.is_equal).then_inc(t_step, 1)
                                for r in range(R):
                                    dve.wait_ge(t_step, n + r + 1)
                                    v.tensor_tensor(hit4[:, r], hit4[:, r],
                                                    keys_of[:, r, side, :].unsqueeze(1).to_broadcast([P, PK, PK]),
                                                    ALU.mult).then_inc(t_step, 1)
                                dve.wait_ge(t_step, n + 2 * R)
                                v.tensor_reduce(key_of[:, side, :, :].rearrange("p r k -> p (r k)"),
                                                hit[:, :, :].rearrange("p r (k a) -> p (r k) a", k=PK),
                                                AX.X, ALU.add).then_inc(t_step, 1)
                                n += 2 * R + 1
                            dve.wait_ge(t_step, n)
                            v.scalar_tensor_tensor(out=idx_f[:, :], in0=key_of[:, 0, :, :].rearrange("p r k -> p (r k)"),
                                                   scalar=float(PN), in1=key_of[:, 1, :, :].rearrange("p r k -> p (r k)"),
                                                   op0=ALU.mult, op1=ALU.add).then_inc(t_step, 1)
                            dve.wait_ge(t_exp, 1)
                            v.tensor_reduce(total[:, :], expd[:, :, :], AX.X, ALU.add).then_inc(t_step, 1)
                            dve.wait_ge(t_step, n + 1)
                            v.tensor_copy(flat(experts), idx_f[:, :]).then_inc(t_step, 1)
                            dve.wait_ge(t_step, n + 2)
                            v.reciprocal(inv[:, :], total[:, :]).then_inc(t_step, 1)
                            dve.wait_ge(t_step, n + 4)
                            v.tensor_tensor(gates[:, :, :].rearrange("p t (h k) -> p (t h) k", h=PH), expd[:, :, :],
                                            inv[:, :].unsqueeze(2).to_broadcast([P, R, PK]), ALU.mult).then_inc(t_step, 1)

            c = ExitStack()
            with c:
                NB, PL = 8, PH * PK
                rows = [sb(c, f"g_rows{i}", [P, D]) for i in range(NB)]
                place = sb(c, "g_place", [P, NB], U32)
                dots = sb(c, "g_dots", [P, TB, PL])
                act_g = sb(c, "g_act", [P, TB, PL])
                weight = sb(c, "g_weight", [P, TB, PL])
                product = sb(c, "g_product", [P, D])
                wide = sb(c, "g_wide", [P, D])
                ssq = sb(c, "g_ssq", [P, TB])
                std = sb(c, "g_std", [P, TB])
                rstd = sb(c, "g_rstd", [P, TB])
                g_full = [sem(f"g_full{i}") for i in range(NB)]
                g_used = sem("g_used")
                g_gelu = sem("g_gelu")
                g_weight = sem("g_weighted")
                g_wide = sem("g_wide_in")
                g_ssq = sem("g_ssq")
                g_std = sem("g_std")
                g_rstd = sem("g_rstd")
                g_norm = sem("g_norm")
                g_out = sem("g_out")
                tables = (peer_down[0], peer_up[0])
                with nc.Block() as block:
                    @block.gpsimd
                    def _(pool):
                        for part in range(2 * TB):
                            tb, table = part // 2, tables[part % 2]

                            def batch(b, free):
                                n0 = part * PL + b * NB
                                for i in range(NB):
                                    if free:
                                        pool.wait_ge(g_used, n0 + i - NB + 1)
                                    pool.tensor_copy(place[:, i:i + 1],
                                                     experts[:, tb, ds(b * NB + i, 1)])
                                    pool.drain()
                                    pool.indirect_dma_start(
                                        out=rows[i][:, :], out_offset=None, in_=table,
                                        in_offset=bass.IndirectOffsetOnAxis(ap=place[:, i:i + 1], axis=0)
                                    ).then_inc(g_full[i], 16)
                            if part == 0:
                                batch(0, False)
                                with pool.Fori(1, PL // NB) as b:
                                    batch(b, True)
                            else:
                                with pool.Fori(0, PL // NB) as b:
                                    batch(b, True)

                    @block.vector
                    def _(dve):
                        for part in range(2 * TB):
                            tb = part // 2
                            if part % 2:
                                dve.wait_ge(g_gelu, tb + 1)
                                nc.vector.tensor_tensor(weight[:, tb, :], act_g[:, tb, :], gates[:, tb, :],
                                                        ALU.mult).then_inc(g_weight, 1)
                                dve.wait_ge(g_weight, tb + 1)
                            with dve.Fori(0, PL // NB) as b:
                                for i in range(NB):
                                    n = part * PL + b * NB + i
                                    dve.wait_ge(g_full[i], (part * (PL // NB) + b + 1) * 16)
                                    if part % 2 == 0:
                                        nc.vector.scalar_tensor_tensor(
                                            out=rows[i][:, :], in0=rows[i][:, :], scalar=1.0, in1=n2[:, tb, :],
                                            op0=ALU.mult, op1=ALU.mult,
                                            accum_out=dots[:, tb, ds(b * NB + i, 1)]).then_inc(g_used, 1)
                                    else:
                                        dve.wait_ge(g_used, n)
                                        nc.vector.scalar_tensor_tensor(
                                            out=acc[:, tb, :], in0=rows[i][:, :],
                                            scalar=weight[:, tb, ds(b * NB + i, 1)], in1=acc[:, tb, :],
                                            op0=ALU.mult, op1=ALU.add).then_inc(g_used, 1)
                        for tb in range(TB):
                            dve.wait_ge(g_std, tb + 1)
                            nc.vector.reciprocal(rstd[:, tb:tb + 1], std[:, tb:tb + 1]).then_inc(g_rstd, 1)
                            dve.wait_ge(g_rstd, tb + 1)
                            dve.wait_ge(g_wide, 16)
                            nc.vector.scalar_tensor_tensor(out=n2[:, tb, :], in0=acc[:, tb, :],
                                                           scalar=rstd[:, tb:tb + 1], in1=wide[:, :],
                                                           op0=ALU.mult, op1=ALU.mult).then_inc(g_norm, 1)

                    @block.scalar
                    def _(act):
                        for tb in range(TB):
                            act.wait_ge(g_used, (2 * tb + 1) * PL)
                            nc.scalar.activation(act_g[:, tb, :], dots[:, tb, :], ACT.Gelu).then_inc(g_gelu, 1)
                        for tb in range(TB):
                            act.wait_ge(g_used, 2 * TB * PL)
                            if tb:
                                act.wait_ge(g_std, tb)
                            nc.scalar.activation(product[:, :], acc[:, tb, :], ACT.Square,
                                                 accum_out=ssq[:, tb:tb + 1]).then_inc(g_ssq, 1)
                            act.wait_ge(g_ssq, tb + 1)
                            nc.scalar.activation(std[:, tb:tb + 1], ssq[:, tb:tb + 1], ACT.Sqrt,
                                                 bias=eps_col[:, 0:1], scale=1.0 / D).then_inc(g_std, 1)

                    @block.sync
                    def _(sp):
                        sp.dma_start(wide[:, :], final_norm_w.rearrange("(o d) -> o d", o=1).to_broadcast([P, D])).then_inc(g_wide, 16)
                        for tb in range(TB):
                            sp.wait_ge(g_norm, tb + 1)
                            sp.dma_start(out[0, tb * P:(tb + 1) * P, :], n2[:, tb, :]).then_inc(g_out, 16)
                        sp.wait_ge(g_out, 16 * TB)




_INS = ['x', 'norm_mix_w', 'w_in', 'conv_a_w', 'ssd_conv_w', 'ssd_conv_b', 'ssd_dt_bias', 'ssd_a_log', 'ssd_d',
        'ssd_norm_w', 'w_branch_a', 'w_branch_b', 'w_branch_c', 'w_out', 'norm_ffn_w', 'peer_w_query',
        'peer_sub_keys', 'peer_down', 'peer_up', 'final_norm_w']


def kernel(**inputs):
    import concourse.bacc as bacc
    from concourse.bass_utils import run_bass_kernel_spmd

    nc = bacc.Bacc("TRN2", target_bir_lowering=False, num_devices=1)
    arrays, args = {}, []
    for name in _INS:
        a = np.ascontiguousarray(inputs[name])
        arrays[f"in_{name}"] = a
        args.append(nc.dram_tensor(f"in_{name}", a.shape, mybir.dt.from_np(a.dtype), kind="ExternalInput").ap())
    args.append(nc.dram_tensor("out_0", (1, T, D), F32, kind="ExternalOutput").ap())
    program(nc, *args)
    return run_bass_kernel_spmd(nc, [arrays], core_ids=[0]).results[0]["out_0"]
```

```python
import numpy as np
import concourse.bass as bass
from concourse import mybir
from contextlib import ExitStack

F32 = mybir.dt.float32
F32R = mybir.dt.float32r
U32 = mybir.dt.uint32
ALU = mybir.AluOpType
ACT = mybir.ActivationFunctionType
AX = mybir.AxisListType
ds = bass.ds

P = 128
D = 2048
T = 256
TB = T // P
KD = D // P
EPS = 1e-6
SBH = 16
SCALE = 128.0 ** -0.5
SSD_W = 4096
GROUPS = 8
HPG = 8
SSD_HEADS = 64
KC = SSD_W // P
COL_A = 0
COL_B = 3 * D
COL_Z = 6 * D
COL_XS = COL_Z + SSD_W
COL_BM = COL_XS + SSD_W
COL_CM = COL_BM + GROUPS * P
COL_DT = COL_CM + GROUPS * P
COL_G = COL_DT + SSD_HEADS
V_NORM = 0
V_FFN = 16
V_CONVA = 32
V_CONVB = 80
V_SSDW = 128
V_SSDN = 320
NEG = -30000.0
PH, PK, PN = 8, 16, 128


def program(nc, x, norm_mix_w, w_in, conv_a_w, ssd_conv_w, ssd_conv_b, ssd_dt_bias, ssd_a_log, ssd_d,
            ssd_norm_w, w_branch_a, w_branch_b, w_branch_c, w_out, norm_ffn_w, peer_w_query,
            peer_sub_keys, peer_down, peer_up, final_norm_w, h_dram, out):
    top = ExitStack()
    with top:
        def sb(ctx, name, shape, dt=F32):
            return ctx.enter_context(nc.sbuf_tensor(name, shape, dt))

        live = []

        def sem(name):
            live.append(nc.alloc_semaphore(name=name))
            return live[-1]

        bank = [top.enter_context(nc.psum_tensor(f"bank{i}", [P, 512], F32)) for i in range(8)]

        ident = sb(top, "ident", [P, P])
        vcols = sb(top, "vcols", [P, 352])
        eps_col = sb(top, "eps_col", [P, 1])

        class Stream:

            def __init__(self, ctx, tag, cols, units, pieces, split=2):
                self.split = split
                self.units = units
                self.pieces = pieces if isinstance(pieces, tuple) else (pieces,) * 4
                self.raw = [sb(ctx, f"{tag}_raw{i}", [P, cols]) for i in range(4)]
                self.hi = [sb(ctx, f"{tag}_hi{i}", [P, cols], F32R) for i in range(split)]
                self.lo = [sb(ctx, f"{tag}_lo{i}", [P, cols], F32R) for i in range(split)]
                self.raw_full = [sem(f"{tag}_raw_full{i}") for i in range(4)]
                self.hi_done = sem(f"{tag}_hi_done")
                self.lo_done = sem(f"{tag}_lo_done")
                self.unit_used = sem(f"{tag}_unit_used")

            def load(self, sp, it, u, first, pairs):
                if not (first and u < 4):
                    sp.wait_ge(self.lo_done, it * self.units + u - 3)
                for dst, src in pairs:
                    sp.dma_start(dst, src).then_inc(self.raw_full[u % 4], 16)

            def split_hi(self, act, it, u, first, cols):
                act.wait_ge(self.raw_full[u % 4], (it * (self.units // 4) + u // 4 + 1) * (16 * self.pieces[u % 4]))
                if not (first and u < self.split):
                    act.wait_ge(self.unit_used, it * self.units + u + 1 - self.split)
                nc.scalar.activation(self.hi[u % self.split][:, 0:cols], self.raw[u % 4][:, 0:cols],
                                     ACT.Copy).then_inc(self.hi_done, 1)

            def split_lo(self, dve, it, u, cols):
                dve.wait_ge(self.hi_done, it * self.units + u + 1)
                nc.vector.tensor_tensor(self.lo[u % self.split][:, 0:cols], self.raw[u % 4][:, 0:cols],
                                        self.hi[u % self.split][:, 0:cols].bitcast(F32),
                                        ALU.subtract).then_inc(self.lo_done, 1)

            def wait_unit(self, pe, it, u):
                pe.wait_ge(self.lo_done, it * self.units + u + 1)

        def tri_matmul(out, lhs, rhs, start, stop):
            nc.tensor.matmul(out, lhs[0], rhs[0], start=start, stop=False, skip_group_check=True)
            nc.tensor.matmul(out, lhs[0], rhs[1], start=False, stop=False, skip_group_check=True)
            return nc.tensor.matmul(out, lhs[1], rhs[0], start=False, stop=stop, skip_group_check=True)

        xT_hi = sb(top, "xT_hi", [P, KD, T], F32R)
        xT_lo = sb(top, "xT_lo", [P, KD, T], F32R)
        gates = sb(top, "gates", [P, TB, PH * PK])
        key_of = sb(top, "key_of", [P, 2, TB * PH * PK])
        trunk = ExitStack()
        acc = sb(trunk, "acc", [P, TB, D])
        mix = ExitStack()
        with mix:
            yT_hi = sb(mix, "yT_hi", [P, KC, T], F32R)
            yT_lo = sb(mix, "yT_lo", [P, KC, T], F32R)

            c = ExitStack()
            with c:
                xt = sb(c, "xt", [P, TB, D])
                junk = sb(c, "junk", [P, D])
                vrows = sb(c, "vrows", [P, 3, P])
                rstd = sb(c, "rstd", [P, TB])
                std = sb(c, "std", [P, TB])
                ssq = sb(c, "ssq", [P, TB])
                p_const = sem("p_const")
                p_vec_in = sem("p_vec_in")
                p_x_in = [sem(f"p_x_in{i}") for i in range(2)]
                p_ssq = sem("p_ssq")
                p_std = sem("p_std")
                p_rstd = sem("p_rstd")
                p_scaled = sem("p_scaled")
                p_vecT = sem("p_vecT")
                p_vcols = sem("p_vcols")
                p_xT = sem("p_xT")
                p_hi = sem("p_hi")
                p_lo = sem("p_lo")
                with nc.Block() as block:
                    @block.sync
                    def _(sp):
                        for tb in range(TB):
                            sp.dma_start(xt[:, tb, :], x[0, tb * P:(tb + 1) * P, :]).then_inc(p_x_in[tb], 16)
                        rows = lambda a, n: a.rearrange("k (c p) -> (k c) p", p=P)
                        cw = ssd_conv_w[0].rearrange("k (c p) -> k c p", p=P)
                        for dst, src in (
                            (vrows[0:16, 0, :], rows(norm_mix_w, 16)),
                            (vrows[16:32, 0, :], rows(norm_ffn_w, 16)),
                            (vrows[80:128, 0, :], rows(ssd_conv_b, 48)),
                            (vrows[64:96, 2, :], rows(ssd_norm_w, 32)),
                            *((vrows[32 + 16 * k:48 + 16 * k, 0, :],
                               conv_a_w[0, k:k + 1, :].rearrange("o (c p) -> (o c) p", p=P)) for k in range(3)),
                            (vrows[0:48, 1, :], cw[0]), (vrows[48:96, 1, :], cw[1]),
                            (vrows[96:128, 1, :], cw[2, 0:32]), (vrows[0:16, 2, :], cw[2, 32:48]),
                            (vrows[16:64, 2, :], cw[3]),
                        ):
                            sp.dma_start(dst, src).then_inc(p_vec_in, 16)

                    @block.gpsimd
                    def _(pool):
                        pool.memset(ident[:, :], 0.0).then_inc(p_const, 1)
                        pool.memset(eps_col[:, :], EPS).then_inc(p_const, 1)
                        pool.wait_ge(p_const, 2)
                        pool.affine_select(out=ident[:, :], in_=ident[:, :], compare_op=ALU.not_equal, fill=1.0,
                                           base=0, pattern=[[-1, P]], channel_multiplier=1).then_inc(p_const, 1)

                    @block.scalar
                    def _(act):
                        act.wait_ge(p_const, 2)
                        for tb in range(TB):
                            act.wait_ge(p_x_in[tb], 16)
                            if tb:
                                act.wait_ge(p_ssq, tb)
                            nc.scalar.activation(junk[:, :], xt[:, tb, :], ACT.Square,
                                                 accum_out=ssq[:, tb:tb + 1]).then_inc(p_ssq, 1)
                        act.wait_ge(p_ssq, TB)
                        nc.scalar.activation(std[:, :], ssq[:, :], ACT.Sqrt, bias=eps_col[:, 0:1],
                                             scale=1.0 / D).then_inc(p_std, 1)
                        act.wait_ge(p_vcols, 1)
                        for k in range(KD):
                            act.wait_ge(p_xT, 2 * (k // 2) + 2)
                            nc.scalar.activation(xT_hi[:, k, :], bank[k // 2][:, (k % 2) * T:(k % 2 + 1) * T],
                                                 ACT.Copy, scale=vcols[:, V_NORM + k:V_NORM + k + 1]).then_inc(p_hi, 1)

                    @block.vector
                    def _(dve):
                        dve.wait_ge(p_vecT, 1)
                        nc.vector.tensor_copy(vcols[:, 0:256], bank[0][:, 0:256])
                        nc.vector.tensor_copy(vcols[:, 256:352], bank[0][:, 256:352]).then_inc(p_vcols, 1)
                        dve.wait_ge(p_std, 1)
                        nc.vector.reciprocal(rstd[:, :], std[:, :]).then_inc(p_rstd, 1)
                        dve.wait_ge(p_rstd, 1)
                        for tb in range(TB):
                            nc.vector.tensor_scalar(xt[:, tb, :], xt[:, tb, :], rstd[:, tb:tb + 1], None,
                                                    ALU.mult).then_inc(p_scaled, 1)
                        for k in range(KD):
                            dve.wait_ge(p_hi, 2 * (k // 2) + 2)
                            nc.vector.scalar_tensor_tensor(
                                out=xT_lo[:, k, :], in0=bank[k // 2][:, (k % 2) * T:(k % 2 + 1) * T],
                                scalar=vcols[:, V_NORM + k:V_NORM + k + 1], in1=xT_hi[:, k, :].bitcast(F32),
                                op0=ALU.mult, op1=ALU.subtract).then_inc(p_lo, 1)

                    @block.tensor
                    def _(pe):
                        pe.wait_ge(p_const, 3)
                        pe.wait_ge(p_vec_in, 16 * 12)
                        nc.tensor.transpose(bank[0][:, 0:128], vrows[:, 0, :], ident[:, :])
                        nc.tensor.transpose(bank[0][:, 128:256], vrows[:, 1, :], ident[:, :])
                        nc.tensor.transpose(bank[0][:, 256:352], vrows[0:96, 2, :], ident[0:96, 0:96]).then_inc(p_vecT, 1)
                        pe.wait_ge(p_vcols, 1)
                        pe.wait_ge(p_scaled, TB)
                        for k in range(KD):
                            for tb in range(TB):
                                at = (k % 2) * T + tb * P
                                last = nc.tensor.transpose(bank[k // 2][:, at:at + P],
                                                           xt[:, tb, k * P:(k + 1) * P], ident[:, :])
                            last.then_inc(p_xT, 1)

            c = ExitStack()
            with c:
                W = 768
                st = Stream(c, "a", 2 * W, 8, 3)
                N_IT = 8
                c_sb = sb(c, "a_c", [P, 512])
                b_sb = sb(c, "a_b", [P, 512])
                gate_hid = sb(c, "a_gate_hid", [P, 2, T + 2])
                y_f = sb(c, "a_y", [P, 2, T])
                a_pad = sem("a_pad")
                a_evac = sem("a_evac")
                a_gh = sem("a_gh")
                a_conv = sem("a_conv")
                a_y = sem("a_y_done")
                a_yhi = sem("a_yhi")
                a_ylo = sem("a_ylo")
                with nc.Block() as block:
                    @block.sync
                    def _(sp):
                        def body(it, first):
                            for u in range(8):
                                raw = st.raw[u % 4][:, :].rearrange("p (k n) -> p k n", k=2)
                                st.load(sp, it, u, first, [
                                    (raw[:, :, i * 256:(i + 1) * 256],
                                     w_in[0, u * 256:(u + 1) * 256, ds(COL_A + i * D + it * 256, 256)].rearrange(
                                         "(k p) n -> p k n", p=P)) for i in range(3)])
                        body(0, True)
                        with sp.Fori(1, N_IT) as it:
                            body(it, False)

                    @block.scalar
                    def _(act):
                        def evacuate(p):
                            act.wait_ge(st.unit_used, 8 * p + 8)
                            nc.scalar.activation(c_sb[:, :], bank[1][:, :], ACT.Copy).then_inc(a_evac, 1)
                            nc.scalar.activation(b_sb[:, :], bank[0][:, :], ACT.Copy).then_inc(a_evac, 1)

                        def y_hi(p):
                            act.wait_ge(a_y, p + 1)
                            nc.scalar.activation(yT_hi[:, ds(2 * p, 2), :], y_f[:, :, :], ACT.Copy).then_inc(a_yhi, 1)

                        def body(it, first):
                            for u in range(8):
                                st.split_hi(act, it, u, first, 2 * W)
                                if not first and u == 0:
                                    evacuate(it - 1)
                                if not first and u == 4:
                                    y_hi(it - 1)
                        body(0, True)
                        with act.Fori(1, N_IT) as it:
                            body(it, False)
                        evacuate(N_IT - 1)
                        y_hi(N_IT - 1)

                    @block.gpsimd
                    def _(pool):
                        pool.memset(gate_hid[:, :, :], 0.0).then_inc(a_pad, 1)

                    @block.vector
                    def _(dve):
                        def gate(p):
                            if isinstance(p, int) and p == 0:
                                dve.wait_ge(a_pad, 1)
                            dve.wait_ge(a_evac, 2 * p + 1)
                            nc.vector.tensor_tensor(gate_hid[:, :, 2:T + 2],
                                                    c_sb[:, :].rearrange("p (j t) -> p j t", j=2),
                                                    bank[2][:, :].rearrange("p (j t) -> p j t", j=2),
                                                    ALU.mult).then_inc(a_gh, 1)

                        def conv(p, j):
                            if j == 0:
                                dve.wait_ge(a_gh, p + 1)
                            w = lambda k: vcols[:, ds(V_CONVA + 16 * k + 2 * p + j, 1)]
                            nc.vector.tensor_scalar(y_f[:, j, :], gate_hid[:, j, 2:T + 2], w(2), None,
                                                    ALU.mult).then_inc(a_conv, 1)
                            for k in (1, 0):
                                dve.wait_ge(a_conv, 6 * p + 3 * j + 2 - k)
                                nc.vector.scalar_tensor_tensor(
                                    out=y_f[:, j, :], in0=gate_hid[:, j, k:k + T], scalar=w(k), in1=y_f[:, j, :],
                                    op0=ALU.mult, op1=ALU.add).then_inc(a_conv, 1)

                        def y(p):
                            dve.wait_ge(a_conv, 6 * p + 6)
                            dve.wait_ge(a_evac, 2 * p + 2)
                            nc.vector.tensor_tensor(y_f[:, :, :], y_f[:, :, :],
                                                    b_sb[:, :].rearrange("p (j t) -> p j t", j=2),
                                                    ALU.mult).then_inc(a_y, 1)

                        def y_lo(p):
                            dve.wait_ge(a_yhi, p + 1)
                            nc.vector.tensor_tensor(yT_lo[:, ds(2 * p, 2), :], y_f[:, :, :],
                                                    yT_hi[:, ds(2 * p, 2), :].bitcast(F32),
                                                    ALU.subtract).then_inc(a_ylo, 1)

                        def body(it, p):
                            for u in range(8):
                                if it is not None:
                                    st.split_lo(dve, it, u, 2 * W)
                                if p is None:
                                    continue
                                if u == 0:
                                    gate(p)
                                if u in (1, 2):
                                    conv(p, u - 1)
                                if u == 3:
                                    y(p)
                                if u == 6:
                                    y_lo(p)
                        body(0, None)
                        body(1, 0)
                        with dve.Fori(2, N_IT) as it:
                            body(it, it - 1)
                        body(None, N_IT - 1)

                    @block.tensor
                    def _(pe):
                        def body(it, first):
                            for u in range(8):
                                st.wait_unit(pe, it, u)
                                for kk in range(2):
                                    k = 2 * u + kk
                                    for m in (2, 3, 0, 1, 4, 5):
                                        if u == 0 and kk == 0 and not first:
                                            if m == 2:
                                                pe.wait_ge(a_evac, 2 * it - 1)
                                            if m == 0:
                                                pe.wait_ge(a_evac, 2 * it)
                                            if m == 4:
                                                pe.wait_ge(a_gh, it)
                                        at = slice(kk * W + m * P, kk * W + (m + 1) * P)
                                        last = tri_matmul(bank[m // 2][:, (m % 2) * T:(m % 2 + 1) * T],
                                                          (st.hi[u % st.split][:, at], st.lo[u % st.split][:, at]),
                                                          (xT_hi[:, k, :], xT_lo[:, k, :]),
                                                          start=k == 0 and m % 2 == 0, stop=k == KD - 1)
                                last.then_inc(st.unit_used, 1)
                        body(0, True)
                        with pe.Fori(1, N_IT) as it:
                            body(it, False)

            def branch(tag, gate_col, w_branch, kb, y0):
                c = ExitStack()
                with c:
                    UN, N_IT = 4 + kb // 4, D // 512
                    add = tag != "ga"
                    st = Stream(c, tag, 4 * 512, UN, 2)
                    sig = sb(c, tag + "_sig", [P, TB, 512])
                    gated = sb(c, tag + "_gated", [P, TB, 512])
                    sig_done = sem(tag + "_sig_done")
                    gated_done = sem(tag + "_gated_done")
                    added = sem(tag + "_added")
                    with nc.Block() as block:
                        @block.sync
                        def _(sp):
                            def body(it, first):
                                for u in range(UN):
                                    raw = st.raw[u % 4][:, :].rearrange("p (k n) -> p k n", k=4)
                                    part = (lambda r: w_in[0, u * 512 + r:u * 512 + r + 256, ds(gate_col + it * 512, 512)]) \
                                        if u < 4 else \
                                        (lambda r: w_branch[0, (u - 4) * 512 + r:(u - 4) * 512 + r + 256, ds(it * 512, 512)])
                                    st.load(sp, it, u, first, [
                                        (raw[:, half * 2:half * 2 + 2, :],
                                         part(half * 256).rearrange("(k p) n -> p k n", p=P)) for half in (1, 0)])
                            body(0, True)
                            with sp.Fori(1, N_IT) as it:
                                body(it, False)

                        @block.scalar
                        def _(act):
                            def body(it, first):
                                for u in range(UN):
                                    st.split_hi(act, it, u, first, 2048)
                                    if u == 5:
                                        act.wait_ge(st.unit_used, it * UN + 4)
                                        if not first:
                                            act.wait_ge(gated_done, 2 * it)
                                        for tb in range(TB):
                                            nc.scalar.activation(sig[:, tb, :], bank[tb][:, :],
                                                                 ACT.Sigmoid).then_inc(sig_done, 1)
                            body(0, True)
                            with act.Fori(1, N_IT) as it:
                                body(it, False)

                        @block.vector
                        def _(dve):
                            def gate(p):
                                dve.wait_ge(st.unit_used, p * UN + UN)
                                dve.wait_ge(sig_done, 2 * p + 2)
                                for tb in range(TB):
                                    dst = gated[:, tb, :] if add else acc[:, tb, ds(p * 512, 512)]
                                    nc.vector.tensor_tensor(dst, sig[:, tb, :], bank[2 + tb][:, :],
                                                            ALU.mult).then_inc(gated_done, 1)
                                if add:
                                    dve.wait_ge(gated_done, 2 * p + 2)
                                    here = acc[:, :, ds(p * 512, 512)]
                                    nc.vector.tensor_tensor(here, here, gated[:, :, :], ALU.add).then_inc(added, 1)

                            def body(it, p):
                                for u in range(UN):
                                    if it is not None:
                                        st.split_lo(dve, it, u, 2048)
                                    if p is not None and u == 0:
                                        gate(p)
                            body(0, None)
                            body(1, 0)
                            with dve.Fori(2, N_IT) as it:
                                body(it, it - 1)
                            gate(N_IT - 1)

                        @block.tensor
                        def _(pe):
                            def body(it, first):
                                for u in range(UN):
                                    if u == 0 and not first:
                                        pe.wait_ge(sig_done, 2 * it)
                                    if u == 4 and not first:
                                        pe.wait_ge(gated_done, 2 * it)
                                    st.wait_unit(pe, it, u)
                                    for kk in range(4):
                                        k = 4 * u + kk if u < 4 else 4 * (u - 4) + kk
                                        at = slice(kk * 512, (kk + 1) * 512)
                                        for tb in range(TB):
                                            t = slice(tb * P, (tb + 1) * P)
                                            lhs = ((xT_hi[:, k, t], xT_lo[:, k, t]) if u < 4 else
                                                   (yT_hi[:, y0 + k, t], yT_lo[:, y0 + k, t]))
                                            last = tri_matmul(bank[tb + (2 if u >= 4 else 0)][:, :], lhs,
                                                              (st.hi[u % st.split][:, at], st.lo[u % st.split][:, at]),
                                                              start=k == 0,
                                                              stop=k == (KD if u < 4 else kb) - 1)
                                    last.then_inc(st.unit_used, 1)
                            body(0, True)
                            with pe.Fori(1, N_IT) as it:
                                body(it, False)

            branch("ga", COL_G, w_branch_a, KD, 0)

            c = ExitStack()
            with c:
                W = 768
                UN, N_IT, PA = 8, 8, 3 * P
                st = Stream(c, "b", 2 * W, UN, 3)
                q_sb = sb(c, "b_q", [P, 2, T])
                k_sb = sb(c, "b_k", [P, 2, T])
                v_sb = sb(c, "b_v", [P, TB, 2 * P])
                mask = sb(c, "b_mask", [P, PA])
                mask_neg = sb(c, "b_mask_neg", [P, PA])
                neg_tri = sb(c, "b_neg_tri", [P, P])
                neg_one = sb(c, "b_neg_one", [P, P])
                z_abs = sb(c, "b_z_abs", [P, 2, PA])
                z_exp = sb(c, "b_z_exp", [P, 2, PA])
                z_ln = sb(c, "b_z_ln", [P, 2, PA])
                splus = sb(c, "b_splus", [P, 2, PA])
                expo = sb(c, "b_expo", [P, 2, PA])
                a_sb = sb(c, "b_a", [P, 2, PA])
                b_const = sem("b_const")
                b_qk = sem("b_qk_copied")
                b_v = sem("b_v_copied")
                b_z = sem("b_z")
                b_abs = sem("b_abs")
                b_e = sem("b_e")
                b_ln = sem("b_ln")
                b_sp1 = sem("b_sp1")
                b_sp = sem("b_sp")
                b_cum = sem("b_cum")
                b_expo = sem("b_expo_done")
                b_a = sem("b_a_done")
                b_o = sem("b_o")
                b_ohi = sem("b_ohi")
                b_olo = sem("b_olo")
                Q, K_, V, Z, O_ = bank[0], bank[1], bank[2], (bank[3], bank[4]), bank[5]
                with nc.Block() as block:
                    @block.sync
                    def _(sp):
                        def body(it, first):
                            for u in range(UN):
                                raw = st.raw[u % 4][:, :].rearrange("p (k n) -> p k n", k=2)
                                st.load(sp, it, u, first, [
                                    (raw[:, :, i * 256:(i + 1) * 256],
                                     w_in[0, u * 256:(u + 1) * 256, ds(COL_B + i * D + it * 256, 256)].rearrange(
                                         "(k p) n -> p k n", p=P)) for i in range(3)])
                        body(0, True)
                        with sp.Fori(1, N_IT) as it:
                            body(it, False)

                    @block.gpsimd
                    def _(pool):
                        pool.memset(mask[:, :], 1.0).then_inc(b_const, 1)
                        pool.memset(mask_neg[:, :], 0.0).then_inc(b_const, 1)
                        pool.memset(neg_tri[:, :], -1.0).then_inc(b_const, 1)
                        pool.memset(neg_one[:, :], -1.0).then_inc(b_const, 1)
                        pool.wait_ge(b_const, 4)
                        for at in (0, 2 * P):
                            for m, fill in ((mask, 0.0), (mask_neg, NEG)):
                                pool.affine_select(out=m[:, at:at + P], in_=m[:, at:at + P], compare_op=ALU.is_ge,
                                                   fill=fill, base=-1, pattern=[[1, P]],
                                                   channel_multiplier=-1).then_inc(b_const, 1)
                        pool.affine_select(out=neg_tri[:, :], in_=neg_tri[:, :], compare_op=ALU.is_ge, fill=0.0,
                                           base=0, pattern=[[-1, P]], channel_multiplier=1).then_inc(b_const, 1)

                    @block.scalar
                    def _(act):
                        def copy_qk(p):
                            act.wait_ge(st.unit_used, UN * p + UN)
                            nc.scalar.activation(q_sb[:, :, :], Q[:, :].rearrange("p (j t) -> p j t", j=2),
                                                 ACT.Copy, scale=SCALE).then_inc(b_qk, 1)
                            nc.scalar.activation(k_sb[:, :, :], K_[:, :].rearrange("p (j t) -> p j t", j=2),
                                                 ACT.Copy).then_inc(b_qk, 1)

                        def softplus(p):
                            for j in range(2):
                                act.wait_ge(b_z, 2 * p + j + 1)
                                nc.scalar.activation(z_abs[:, j, :], Z[j][:, 0:PA], ACT.Abs).then_inc(b_abs, 1)
                            act.wait_ge(b_abs, 2 * p + 2)
                            nc.scalar.activation(z_exp[:, :, :], z_abs[:, :, :], ACT.Exp, scale=-1.0).then_inc(b_e, 1)
                            act.wait_ge(b_e, p + 1)
                            nc.scalar.activation(z_ln[:, :, :], z_exp[:, :, :], ACT.Ln, bias=1.0).then_inc(b_ln, 1)

                        def weights(p):
                            act.wait_ge(b_expo, 2 * p + 2)
                            nc.scalar.activation(a_sb[:, :, :], expo[:, :, :], ACT.Exp).then_inc(b_a, 1)

                        def o_hi(p):
                            act.wait_ge(b_o, p + 1)
                            nc.scalar.activation(yT_hi[:, ds(KD + 2 * p, 2), :],
                                                 O_[:, :].rearrange("p (j t) -> p j t", j=2),
                                                 ACT.Copy).then_inc(b_ohi, 1)

                        def body(it, p):
                            for u in range(UN):
                                if it is not None:
                                    st.split_hi(act, it, u, isinstance(it, int) and it == 0, 2 * W)
                                if p is None:
                                    continue
                                if u == 0:
                                    copy_qk(p)
                                if u == 3:
                                    softplus(p)
                                if u == 6:
                                    weights(p)
                                if u == 7:
                                    o_hi(p)
                        body(0, None)
                        with act.Fori(1, N_IT) as it:
                            body(it, it - 1)
                        body(None, N_IT - 1)

                    @block.vector
                    def _(dve):
                        def copy_v(p):
                            dve.wait_ge(st.unit_used, UN * p + UN)
                            nc.vector.tensor_copy(v_sb[:, :, :], V[:, :].rearrange("p (s d) -> p s d", s=TB)).then_inc(b_v, 1)

                        def softplus(p):
                            dve.wait_ge(b_ln, p + 1)
                            for j in range(2):
                                nc.vector.scalar_tensor_tensor(out=splus[:, j, :], in0=Z[j][:, 0:PA], scalar=0.0,
                                                               in1=z_ln[:, j, :], op0=ALU.max,
                                                               op1=ALU.add).then_inc(b_sp1, 1)
                            for j in range(2):
                                dve.wait_ge(b_sp1, 2 * p + j + 1)
                                nc.vector.tensor_tensor(splus[:, j, :], splus[:, j, :], mask[:, :],
                                                        ALU.mult).then_inc(b_sp, 1)

                        def exponent(p):
                            for j in range(2):
                                dve.wait_ge(b_cum, 2 * p + j + 1)
                                nc.vector.scalar_tensor_tensor(out=expo[:, j, :], in0=Z[j][:, 0:PA], scalar=0.0,
                                                               in1=mask_neg[:, :], op0=ALU.min,
                                                               op1=ALU.add).then_inc(b_expo, 1)

                        def o_lo(p):
                            dve.wait_ge(b_ohi, p + 1)
                            here = ds(KD + 2 * p, 2)
                            nc.vector.tensor_tensor(yT_lo[:, here, :], O_[:, :].rearrange("p (j t) -> p j t", j=2),
                                                    yT_hi[:, here, :].bitcast(F32), ALU.subtract).then_inc(b_olo, 1)

                        def body(it, p):
                            for u in range(UN):
                                if it is not None:
                                    st.split_lo(dve, it, u, 2 * W)
                                if p is None:
                                    continue
                                if u == 0:
                                    copy_v(p)
                                if u == 3:
                                    softplus(p)
                                if u == 6:
                                    exponent(p)
                                if u == 7:
                                    o_lo(p)
                        dve.wait_ge(b_const, 9)
                        body(0, None)
                        with dve.Fori(1, N_IT) as it:
                            body(it, it - 1)
                        body(None, N_IT - 1)

                    @block.tensor
                    def _(pe):
                        mm = lambda out, l, r, start: nc.tensor.matmul(out, l, r, start=start, stop=True,
                                                                       skip_group_check=True)

                        def z(p):
                            pe.wait_ge(b_qk, 2 * p + 2)
                            for j in range(2):
                                if not (isinstance(p, int) and p == 0):
                                    pe.wait_ge(b_expo, 2 * p + j - 1)
                                mm(Z[j][:, 0:T], k_sb[:, j, 0:P], q_sb[:, j, :], True)
                                mm(Z[j][:, T:PA], k_sb[:, j, P:T], q_sb[:, j, P:T], False).then_inc(b_z, 1)

                        def cumulate(p):
                            for j in range(2):
                                pe.wait_ge(b_sp, 2 * p + j + 1)
                                mm(Z[j][:, 0:T], neg_tri[:, :], splus[:, j, 0:T], False)
                                mm(Z[j][:, T:PA], neg_tri[:, :], splus[:, j, T:PA], False)
                                mm(Z[j][:, P:T], neg_one[:, :], splus[:, j, T:PA], False).then_inc(b_cum, 1)

                        def outputs(p):
                            pe.wait_ge(b_a, p + 1)
                            if not (isinstance(p, int) and p == 0):
                                pe.wait_ge(b_olo, p)
                            for j in range(2):
                                d = slice(j * P, (j + 1) * P)
                                mm(O_[:, j * T:(j + 1) * T], v_sb[:, 0, d], a_sb[:, j, 0:T], j == 0)
                                last = mm(O_[:, j * T + P:(j + 1) * T], v_sb[:, 1, d], a_sb[:, j, T:PA], False)
                            last.then_inc(b_o, 1)

                        def body(it, p):
                            for u in range(UN):
                                if it is not None:
                                    st.wait_unit(pe, it, u)
                                    for kk in range(2):
                                        k = 2 * u + kk
                                        xs = (xT_hi[:, k, :], xT_lo[:, k, :])
                                        for m in range(4):
                                            if u == 0 and kk == 0 and p is not None and m % 2 == 0:
                                                pe.wait_ge(b_qk, 2 * it - 1 + m // 2)
                                            at = slice(kk * W + m * P, kk * W + (m + 1) * P)
                                            tri_matmul(bank[m // 2][:, (m % 2) * T:(m % 2 + 1) * T],
                                                       (st.hi[u % st.split][:, at], st.lo[u % st.split][:, at]), xs,
                                                       start=k == 0 and m % 2 == 0, stop=k == KD - 1)
                                        if u == 0 and kk == 0 and p is not None:
                                            pe.wait_ge(b_v, it)
                                        at = slice(kk * W + 512, kk * W + W)
                                        for tb in range(TB):
                                            t = slice(tb * P, (tb + 1) * P)
                                            last = tri_matmul(V[:, tb * T:(tb + 1) * T],
                                                              (xT_hi[:, k, t], xT_lo[:, k, t]),
                                                              (st.hi[u % st.split][:, at], st.lo[u % st.split][:, at]),
                                                              start=k == 0 and tb == 0, stop=k == KD - 1)
                                    last.then_inc(st.unit_used, 1)
                                if p is None:
                                    continue
                                if u == 1:
                                    z(p)
                                if u == 4:
                                    cumulate(p)
                                if u == 6:
                                    outputs(p)
                        pe.wait_ge(b_const, 9)
                        body(0, None)
                        body(1, 0)
                        with pe.Fori(2, N_IT) as it:
                            body(it, it - 1)
                        body(None, N_IT - 1)
            branch("gb", COL_G + D, w_branch_b, KD, KD)

            ssd = ExitStack()
            with ssd:
                upper = sb(ssd, "upper", [P, P])
                neg_upper = sb(ssd, "neg_upper", [P, P])
                ones = sb(ssd, "ones", [P, P])
                dt = sb(ssd, "dt", [P, TB, SSD_HEADS])
                da = sb(ssd, "da", [P, TB, SSD_HEADS])
                decay = sb(ssd, "decay", [P, SSD_HEADS])
                d_col = sb(ssd, "d_col", [P, KC])

                c = ExitStack()
                with c:
                    n_dt = KD * SSD_HEADS
                    w_raw = sb(c, "dt_w_raw", [P, n_dt])
                    w_hi = sb(c, "dt_w_hi", [P, n_dt], F32R)
                    w_lo = sb(c, "dt_w_lo", [P, n_dt], F32R)
                    bias = sb(c, "dt_bias", [P, SSD_HEADS])
                    a_log = sb(c, "dt_a_log", [P, SSD_HEADS])
                    a_neg = sb(c, "dt_a_exp", [P, SSD_HEADS])
                    below = sb(c, "dt_below", [P, P])
                    u = sb(c, "dt_u", [P, TB, SSD_HEADS])
                    u_abs = sb(c, "dt_u_abs", [P, TB, SSD_HEADS])
                    u_exp = sb(c, "dt_u_exp", [P, TB, SSD_HEADS])
                    u_ln = sb(c, "dt_u_ln", [P, TB, SSD_HEADS])
                    d_w = sem("d_w")
                    d_vec = sem("d_vec")
                    d_const = sem("d_const")
                    d_hi = sem("d_hi")
                    d_lo = sem("d_lo")
                    d_proj = sem("d_proj")
                    d_u = sem("d_u")
                    d_act = sem("d_act")
                    d_dt = sem("d_dt")
                    d_da = sem("d_da")
                    d_dec = sem("d_dec")
                    d_out = sem("d_out")
                    with nc.Block() as block:
                        @block.sync
                        def _(sp):
                            sp.dma_start(w_raw[:, :].rearrange("p (k n) -> p k n", k=KD),
                                         w_in[0, :, COL_DT:COL_DT + SSD_HEADS].rearrange(
                                             "(k p) n -> p k n", p=P)).then_inc(d_w, 16)
                            sp.dma_start(bias[:, :], ssd_dt_bias[0:1, :].to_broadcast([P, SSD_HEADS])).then_inc(d_vec, 16)
                            sp.dma_start(a_log[:, :], ssd_a_log[0:1, :].to_broadcast([P, SSD_HEADS])).then_inc(d_vec, 16)
                            heads = ssd_d.rearrange("o (c h) -> h (o c)", h=2)
                            for h in range(2):
                                sp.dma_start(d_col[64 * h:64 * h + 64, :],
                                             heads[h:h + 1, :].to_broadcast([64, KC]),
                                             allow_slow_non_contiguous=True).then_inc(d_vec, 16)

                        @block.gpsimd
                        def _(pool):
                            pool.memset(ones[:, :], 1.0).then_inc(d_const, 1)
                            pool.memset(upper[:, :], 1.0).then_inc(d_const, 1)
                            pool.memset(neg_upper[:, :], -1.0).then_inc(d_const, 1)
                            pool.memset(below[:, :], 1.0).then_inc(d_const, 1)
                            pool.wait_ge(d_const, 4)
                            for m in (upper, neg_upper):
                                pool.affine_select(out=m[:, :], in_=m[:, :], compare_op=ALU.is_ge, fill=0.0, base=0,
                                                   pattern=[[1, P]], channel_multiplier=-1).then_inc(d_const, 1)
                            pool.affine_select(out=below[:, :], in_=below[:, :], compare_op=ALU.is_ge, fill=0.0,
                                               base=-1, pattern=[[-1, P]], channel_multiplier=1).then_inc(d_const, 1)

                        @block.scalar
                        def _(act):
                            act.wait_ge(d_w, 16)
                            nc.scalar.activation(w_hi[:, :], w_raw[:, :], ACT.Copy).then_inc(d_hi, 1)
                            act.wait_ge(d_vec, 64)
                            nc.scalar.activation(a_neg[:, :], a_log[:, :], ACT.Exp).then_inc(d_act, 1)
                            act.wait_ge(d_u, 1)
                            nc.scalar.activation(u_abs[:, :, :], u[:, :, :], ACT.Abs).then_inc(d_act, 1)
                            act.wait_ge(d_act, 2)
                            nc.scalar.activation(u_exp[:, :, :], u_abs[:, :, :], ACT.Exp, scale=-1.0).then_inc(d_act, 1)
                            act.wait_ge(d_act, 3)
                            nc.scalar.activation(u_ln[:, :, :], u_exp[:, :, :], ACT.Ln, bias=1.0).then_inc(d_act, 1)
                            act.wait_ge(d_dec, 1)
                            nc.scalar.activation(decay[:, :], bank[1][:, 0:SSD_HEADS], ACT.Exp).then_inc(d_out, 1)

                        @block.vector
                        def _(dve):
                            dve.wait_ge(d_hi, 1)
                            nc.vector.tensor_tensor(w_lo[:, :], w_raw[:, :], w_hi[:, :].bitcast(F32),
                                                    ALU.subtract).then_inc(d_lo, 1)
                            dve.wait_ge(d_vec, 64)
                            dve.wait_ge(d_proj, 1)
                            for tb in range(TB):
                                last = nc.vector.tensor_tensor(u[:, tb, :],
                                                               bank[0][:, tb * SSD_HEADS:(tb + 1) * SSD_HEADS],
                                                               bias[:, :], ALU.add)
                            last.then_inc(d_u, 1)
                            dve.wait_ge(d_act, 4)
                            nc.vector.scalar_tensor_tensor(out=dt[:, :, :], in0=u[:, :, :], scalar=0.0,
                                                           in1=u_ln[:, :, :], op0=ALU.max, op1=ALU.add).then_inc(d_dt, 1)
                            dve.wait_ge(d_dt, 1)
                            for tb in range(TB):
                                last = nc.vector.scalar_tensor_tensor(out=da[:, tb, :], in0=dt[:, tb, :], scalar=-1.0,
                                                                      in1=a_neg[:, :], op0=ALU.mult, op1=ALU.mult)
                            last.then_inc(d_da, 1)

                        @block.tensor
                        def _(pe):
                            pe.wait_ge(d_lo, 1)
                            for k in range(KD):
                                at = slice(k * SSD_HEADS, (k + 1) * SSD_HEADS)
                                for tb in range(TB):
                                    t = slice(tb * P, (tb + 1) * P)
                                    last = tri_matmul(bank[0][:, tb * SSD_HEADS:(tb + 1) * SSD_HEADS],
                                                      (xT_hi[:, k, t], xT_lo[:, k, t]), (w_hi[:, at], w_lo[:, at]),
                                                      start=k == 0 and tb == 0, stop=k == KD - 1)
                            last.then_inc(d_proj, 1)
                            pe.wait_ge(d_const, 7)
                            pe.wait_ge(d_da, 1)
                            nc.tensor.matmul(bank[1][:, 0:SSD_HEADS], below[:, :], da[:, 0, :],
                                             start=True, stop=True).then_inc(d_dec, 1)

                c = ExitStack()
                with c:
                    W, UN, N_IT = 1280, 16, GROUPS
                    st = Stream(c, "c", W, UN, 4)
                    zs = sb(c, "c_zs", [P, 4, T])
                    xpad = sb(c, "c_xpad", [P, 6, T + 3])
                    xc = sb(c, "c_xc", [P, 6, T])
                    b_tok = sb(c, "c_b_tok", [P, P])
                    cbm = sb(c, "c_cbm", [P, TB, P])
                    xdt = sb(c, "c_xdt", [P, TB, 512])
                    xdd = sb(c, "c_xdd", [P, 512])
                    dag = sb(c, "c_dag", [P, TB, HPG])
                    wts = sb(c, "c_wts", [P, TB, HPG, P])
                    ce = sb(c, "c_ce", [P, HPG, P])
                    sq = ce[:, :, :].rearrange("p a b -> p (a b)").rearrange("p (a b) -> p a b", a=4)
                    prev = sb(c, "c_prev", [P, 512])
                    yz = sb(c, "c_yz", [P, 4, T])
                    rs_ln = sb(c, "c_rs_ln", [P, T])
                    rs = sb(c, "c_rs", [P, T])
                    s = {n: sem("c_" + n) for n in (
                        "pad", "evac", "conv", "xc", "tr", "btok", "cbm", "xdt", "dag", "diff", "min", "exp", "wts",
                        "cs", "ecs", "prev", "ce", "y", "skip", "yz", "sq", "sum", "rsl", "rs", "yn", "yhi", "ylo")}
                    first_p = lambda p: isinstance(p, int) and p == 0
                    with nc.Block() as block:
                        @block.sync
                        def _(sp):
                            def body(it, first):
                                for u in range(UN):
                                    raw = st.raw[u % 4]
                                    r = slice(u * P, (u + 1) * P)
                                    st.load(sp, it, u, first, [
                                        (raw[:, 512:1024], w_in[0, r, ds(COL_XS + it * 512, 512)]),
                                        (raw[:, 0:512], w_in[0, r, ds(COL_Z + it * 512, 512)]),
                                        (raw[:, 1024:1152], w_in[0, r, ds(COL_BM + it * P, P)]),
                                        (raw[:, 1152:1280], w_in[0, r, ds(COL_CM + it * P, P)])])
                            body(0, True)
                            with sp.Fori(1, N_IT) as it:
                                body(it, False)

                        @block.gpsimd
                        def _(pool):
                            pool.memset(xpad[:, :, :], 0.0).then_inc(s["pad"], 1)

                            def scale_c(p):
                                pool.wait_ge(s["ecs"], 2 * p + 2)
                                pool.tensor_tensor(ce[:, :, :], ce[:, :, :],
                                                   xc[:, 5:6, P:T].to_broadcast([P, HPG, P]),
                                                   ALU.mult).then_inc(s["ce"], 1)
                            scale_c(0)
                            with pool.Fori(1, N_IT) as p:
                                scale_c(p)

                        @block.scalar
                        def _(act):
                            def evacuate(p):
                                act.wait_ge(st.unit_used, UN * p + UN)
                                if first_p(p):
                                    act.wait_ge(s["pad"], 1)
                                for i in range(3):
                                    nc.scalar.activation(xpad[:, 2 * i:2 * i + 2, 3:T + 3],
                                                         bank[2 + i][:, :].rearrange("p (j t) -> p j t", j=2),
                                                         ACT.Copy).then_inc(s["evac"], 1)
                                for i in range(2):
                                    nc.scalar.activation(zs[:, 2 * i:2 * i + 2, :],
                                                         bank[i][:, :].rearrange("p (j t) -> p j t", j=2),
                                                         ACT.Silu).then_inc(s["evac"], 1)

                            def silu_x(p):
                                act.wait_ge(s["conv"], 24 * p + 24)
                                nc.scalar.activation(xc[:, :, :], xc[:, :, :], ACT.Silu).then_inc(s["xc"], 1)

                            def b_tokens(p):
                                act.wait_ge(s["tr"], 3 * p + 3)
                                nc.scalar.activation(b_tok[:, :], bank[7][:, 0:P], ACT.Copy).then_inc(s["btok"], 1)

                            def exp_w(p, ch):
                                for q in range(2):
                                    act.wait_ge(s["min"], 4 * p + 2 * ch + q + 1)
                                    here = wts[:, ch, 4 * q:4 * q + 4, :]
                                    nc.scalar.activation(here, here, ACT.Exp).then_inc(s["exp"], 1)

                            def exp_cs(p):
                                for q in range(2):
                                    act.wait_ge(s["cs"], 3 * p + q + 1)
                                    nc.scalar.activation(ce[:, 4 * q:4 * q + 4, :],
                                                         bank[5 + q][:, :].rearrange("p (h l) -> p h l", h=4),
                                                         ACT.Exp).then_inc(s["ecs"], 1)
                                act.wait_ge(s["cs"], 3 * p + 3)
                                nc.scalar.activation(prev[:, :], bank[7][:, :], ACT.Copy).then_inc(s["prev"], 1)

                            def square(p):
                                act.wait_ge(s["yz"], p + 1)
                                nc.scalar.activation(sq, yz[:, :, :], ACT.Square).then_inc(s["sq"], 1)

                            def inv_rms(r):
                                act.wait_ge(s["sum"], r + 1)
                                nc.scalar.activation(rs_ln[:, :], bank[7][:, 0:T], ACT.Ln, bias=eps_col[:, 0:1],
                                                     scale=1.0 / 512).then_inc(s["rsl"], 1)
                                act.wait_ge(s["rsl"], r + 1)
                                nc.scalar.activation(rs[:, :], rs_ln[:, :], ACT.Exp, scale=-0.5).then_inc(s["rs"], 1)

                            def y_hi(r):
                                act.wait_ge(s["yn"], 4 * r + 4)
                                nc.scalar.activation(yT_hi[:, ds(4 * r, 4), :], yz[:, :, :], ACT.Copy).then_inc(s["yhi"], 1)

                            def body(it, p, r):
                                for u in range(UN):
                                    if it is not None:
                                        st.split_hi(act, it, u, first_p(it), W)
                                    if p is not None:
                                        if u == 0:
                                            evacuate(p)
                                        if u == 6:
                                            silu_x(p)
                                        if u == 8:
                                            b_tokens(p)
                                        if u == 10:
                                            exp_w(p, 0)
                                        if u == 12:
                                            exp_w(p, 1)
                                        if u == 13:
                                            exp_cs(p)
                                        if u == 15:
                                            square(p)
                                    if r is not None:
                                        if u == 1:
                                            inv_rms(r)
                                        if u == 7:
                                            y_hi(r)
                            body(0, None, None)
                            body(1, 0, None)
                            with act.Fori(2, N_IT) as it:
                                body(it, it - 1, it - 2)
                            body(None, N_IT - 1, N_IT - 2)
                            body(None, None, N_IT - 1)

                        @block.vector
                        def _(dve):
                            def conv(p, b):
                                dve.wait_ge(s["evac"], 5 * p + b // 2 + 1)
                                ch = 4 * p + b if b < 4 else (32 + p if b == 4 else 40 + p)
                                w = lambda k: vcols[:, ds(V_SSDW + 48 * k + ch, 1)]
                                nc.vector.tensor_scalar(xc[:, b, :], xpad[:, b, 3:T + 3], w(3),
                                                        vcols[:, ds(V_CONVB + ch, 1)], ALU.mult,
                                                        ALU.add).then_inc(s["conv"], 1)
                                for k in (2, 1, 0):
                                    dve.wait_ge(s["conv"], 24 * p + 4 * b + 3 - k)
                                    nc.vector.scalar_tensor_tensor(
                                        out=xc[:, b, :], in0=xpad[:, b, k:k + T], scalar=w(k), in1=xc[:, b, :],
                                        op0=ALU.mult, op1=ALU.add).then_inc(s["conv"], 1)

                            def per_head(a):
                                return a.unsqueeze(2).to_broadcast([P, HPG, 64])

                            def tokens(p):
                                here = ds(HPG * p, HPG)
                                nc.vector.tensor_copy(dag[:, :, :], da[:, :, here]).then_inc(s["dag"], 1)
                                for tb in range(TB):
                                    dve.wait_ge(s["tr"], 3 * p + tb + 1)
                                    nc.vector.tensor_tensor(xdt[:, tb, :].rearrange("p (h d) -> p h d", h=HPG),
                                                            bank[5 + tb][:, :].rearrange("p (h d) -> p h d", h=HPG),
                                                            per_head(dt[:, tb, here]), ALU.mult).then_inc(s["xdt"], 1)
                                dve.wait_ge(s["xdt"], 2 * p + 1)
                                nc.vector.tensor_tensor(xdd[:, :].rearrange("p (h d) -> p h d", h=HPG),
                                                        xdt[:, 0, :].rearrange("p (h d) -> p h d", h=HPG),
                                                        per_head(decay[:, here]), ALU.mult)
                                dve.wait_ge(s["btok"], p + 1)
                                for ch in range(TB):
                                    nc.vector.tensor_tensor(cbm[:, ch, :], bank[7][:, P + ch * P:2 * P + ch * P],
                                                            upper[:, :], ALU.mult).then_inc(s["cbm"], 1)

                            def clamp(p, ch):
                                for q in range(2):
                                    dve.wait_ge(s["diff"], 4 * p + 2 * ch + q + 1)
                                    nc.vector.tensor_scalar(wts[:, ch, 4 * q:4 * q + 4, :],
                                                            bank[5 + q][:, :].rearrange("p (h l) -> p h l", h=4),
                                                            0.0, None, ALU.min).then_inc(s["min"], 1)

                            def weights(p, ch):
                                for q in range(2):
                                    dve.wait_ge(s["exp"], 4 * p + 2 * ch + q + 1)
                                    here = wts[:, ch, 4 * q:4 * q + 4, :]
                                    nc.vector.tensor_tensor(here, here, cbm[:, ch:ch + 1, :].to_broadcast([P, 4, P]),
                                                            ALU.mult).then_inc(s["wts"], 1)

                            def skip_gate(p):
                                for j in range(4):
                                    dve.wait_ge(s["y"], 2 * p + j // 2 + 1)
                                    nc.vector.scalar_tensor_tensor(
                                        out=yz[:, j, :], in0=xc[:, j, :], scalar=d_col[:, ds(4 * p + j, 1)],
                                        in1=bank[5 + j // 2][:, (j % 2) * T:(j % 2 + 1) * T],
                                        op0=ALU.mult, op1=ALU.add).then_inc(s["skip"], 1)
                                dve.wait_ge(s["skip"], 4 * p + 4)
                                nc.vector.tensor_tensor(yz[:, :, :], yz[:, :, :], zs[:, :, :], ALU.mult).then_inc(s["yz"], 1)

                            def normalise(r):
                                dve.wait_ge(s["rs"], r + 1)
                                for j in range(4):
                                    nc.vector.scalar_tensor_tensor(
                                        out=yz[:, j, :], in0=yz[:, j, :], scalar=vcols[:, ds(V_SSDN + 4 * r + j, 1)],
                                        in1=rs[:, :], op0=ALU.mult, op1=ALU.mult).then_inc(s["yn"], 1)

                            def y_lo(r):
                                dve.wait_ge(s["yhi"], r + 1)
                                here = ds(4 * r, 4)
                                nc.vector.tensor_tensor(yT_lo[:, here, :], yz[:, :, :], yT_hi[:, here, :].bitcast(F32),
                                                        ALU.subtract).then_inc(s["ylo"], 1)

                            def body(it, p, r):
                                for u in range(UN):
                                    if it is not None:
                                        st.split_lo(dve, it, u, W)
                                    if p is not None and u < 6:
                                        conv(p, u)
                                    if r is not None:
                                        if u == 6:
                                            normalise(r)
                                        if u == 7:
                                            y_lo(r)
                                    if p is not None:
                                        if u == 8:
                                            tokens(p)
                                        if u == 10:
                                            clamp(p, 0)
                                        if u == 12:
                                            clamp(p, 1)
                                            weights(p, 0)
                                        if u == 13:
                                            weights(p, 1)
                                        if u == 15:
                                            skip_gate(p)
                            body(0, None, None)
                            body(1, 0, None)
                            with dve.Fori(2, N_IT) as it:
                                body(it, it - 1, it - 2)
                            body(None, N_IT - 1, N_IT - 2)
                            body(None, None, N_IT - 1)

                        @block.tensor
                        def _(pe):
                            mm = lambda out, l, r, start: nc.tensor.matmul(out, l, r, start=start, stop=True,
                                                                           skip_group_check=True)

                            def turn(p):
                                pe.wait_ge(s["xc"], p + 1)
                                if not first_p(p):
                                    pe.wait_ge(s["yz"], p)
                                    pe.wait_ge(s["rsl"], p)
                                for tb in range(TB):
                                    t = slice(tb * P, (tb + 1) * P)
                                    for j in range(4):
                                        last = nc.tensor.transpose(bank[5 + tb][:, j * P:(j + 1) * P],
                                                                   xc[:, j, t], ident[:, :])
                                    last.then_inc(s["tr"], 1)
                                nc.tensor.transpose(bank[7][:, 0:P], xc[:, 4, 0:P], ident[:, :])
                                for ch in range(TB):
                                    t = slice(ch * P, (ch + 1) * P)
                                    last = mm(bank[7][:, P + ch * P:2 * P + ch * P], xc[:, 4, t], xc[:, 5, t], True)
                                last.then_inc(s["tr"], 1)

                            def bcast(ch, h):
                                return dag[:, ch, h:h + 1].to_broadcast([P, P])

                            def diffs(p, ch):
                                if ch == 0:
                                    pe.wait_ge(s["dag"], p + 1)
                                    pe.wait_ge(s["xdt"], 2 * p + 2)
                                else:
                                    pe.wait_ge(s["min"], 4 * p + 2)
                                for q in range(2):
                                    for h in range(4):
                                        mm(bank[5 + q][:, h * P:(h + 1) * P], bcast(ch, 4 * q + h), upper[:, :], h == 0)
                                    mm(bank[5 + q][:, :].rearrange("p (h l) -> p h l", h=4), neg_upper[:, :],
                                       dag[:, ch, 4 * q:4 * q + 4].unsqueeze(2).to_broadcast([P, 4, P]),
                                       False).then_inc(s["diff"], 1)

                            def sums_states(p):
                                pe.wait_ge(s["min"], 4 * p + 4)
                                for q in range(2):
                                    for h in range(4):
                                        last = mm(bank[5 + q][:, h * P:(h + 1) * P], bcast(1, 4 * q + h), upper[:, :], h == 0)
                                    last.then_inc(s["cs"], 1)
                                pe.wait_ge(s["cbm"], 2 * p + 2)
                                mm(bank[7][:, :], b_tok[:, :], xdd[:, :], True).then_inc(s["cs"], 1)

                            def outputs(p):
                                pe.wait_ge(s["wts"], 4 * p + 4)
                                pe.wait_ge(s["ce"], p + 1)
                                pe.wait_ge(s["prev"], p + 1)
                                for i in range(2):
                                    for j in (2 * i, 2 * i + 1):
                                        for hh in range(2):
                                            h = 2 * j + hh
                                            rows = slice(64 * hh, 64 * hh + 64)
                                            o = lambda ch: bank[5 + i][rows, (j % 2) * T + ch * P:(j % 2) * T + ch * P + P]
                                            x_of = slice(64 * h, 64 * h + 64)
                                            mm(o(0), xdt[:, 0, x_of], wts[:, 0, h, :], True)
                                            mm(o(1), xdt[:, 1, x_of], wts[:, 1, h, :], True)
                                            last = mm(o(1), prev[:, x_of], ce[:, h, :], False)
                                    last.then_inc(s["y"], 1)

                            def square_sum(p):
                                pe.wait_ge(s["sq"], p + 1)
                                for j in range(4):
                                    last = mm(bank[7][:, 0:T], ones[:, :], sq[:, j, :], j == 0)
                                last.then_inc(s["sum"], 1)

                            def body(it, p):
                                for u in range(UN):
                                    if it is not None:
                                        st.wait_unit(pe, it, u)
                                        xs = (xT_hi[:, u, :], xT_lo[:, u, :])
                                        for i, m in enumerate((4, 5, 6, 7, 8, 9, 0, 1, 2, 3)):
                                            if u == 0 and p is not None and i % 2 == 0:
                                                pe.wait_ge(s["evac"], 5 * p + i // 2 + 1)
                                            at = slice(m * P, (m + 1) * P)
                                            last = tri_matmul(bank[m // 2][:, (m % 2) * T:(m % 2 + 1) * T],
                                                              (st.hi[u % st.split][:, at], st.lo[u % st.split][:, at]), xs,
                                                              start=u == 0 and m % 2 == 0, stop=u == KD - 1)
                                        last.then_inc(st.unit_used, 1)
                                    if p is None:
                                        continue
                                    if u == 6:
                                        turn(p)
                                    if u == 8:
                                        diffs(p, 0)
                                    if u == 10:
                                        diffs(p, 1)
                                    if u == 12:
                                        sums_states(p)
                                    if u == 13:
                                        outputs(p)
                                    if u == 15:
                                        square_sum(p)
                            body(0, None)
                            body(1, 0)
                            with pe.Fori(2, N_IT) as it:
                                body(it, it - 1)
                            body(None, N_IT - 1)
            branch("gc", COL_G + 2 * D, w_branch_c, KC, 0)

            c = ExitStack()
            with c:
                UN, N_IT = 4, D // 512
                st = Stream(c, "o", 4 * 512, UN, 2)
                o_tr = sem("o_tr")
                o_hi = sem("o_hi")
                o_lo = sem("o_lo")
                o_x = sem("o_x")
                o_h = sem("o_h")
                with nc.Block() as block:
                    @block.sync
                    def _(sp):
                        def body(it, first):
                            for u in range(UN):
                                raw = st.raw[u][:, :].rearrange("p (k n) -> p k n", k=4)
                                st.load(sp, it, u, first, [
                                    (raw[:, half * 2:half * 2 + 2, :],
                                     w_out[0, u * 512 + half * 256:u * 512 + half * 256 + 256,
                                           ds(it * 512, 512)].rearrange("(k p) n -> p k n", p=P)) for half in (1, 0)])
                        body(0, True)
                        sp.wait_ge(o_tr, KD)
                        for tb in range(TB):
                            sp.dma_start(acc[:, tb, :], x[0, tb * P:(tb + 1) * P, :]).then_inc(o_x, 16)
                        with sp.Fori(1, N_IT) as it:
                            body(it, False)

                    @block.scalar
                    def _(act):
                        for k in range(KD):
                            act.wait_ge(o_tr, 2 * (k // 2) + 2)
                            nc.scalar.activation(yT_hi[:, k, :], bank[2 + (k // 2) % 4][:, (k % 2) * T:(k % 2 + 1) * T],
                                                 ACT.Copy).then_inc(o_hi, 1)

                        def body(it, first):
                            for u in range(UN):
                                st.split_hi(act, it, u, first, 2048)
                        body(0, True)
                        with act.Fori(1, N_IT) as it:
                            body(it, False)

                    @block.vector
                    def _(dve):
                        for k in range(KD):
                            dve.wait_ge(o_hi, 2 * (k // 2) + 2)
                            nc.vector.tensor_tensor(yT_lo[:, k, :], bank[2 + (k // 2) % 4][:, (k % 2) * T:(k % 2 + 1) * T],
                                                    yT_hi[:, k, :].bitcast(F32), ALU.subtract).then_inc(o_lo, 1)

                        def residual(p):
                            dve.wait_ge(st.unit_used, UN * p + UN)
                            if isinstance(p, int):
                                dve.wait_ge(o_x, 16 * TB)
                            for tb in range(TB):
                                here = acc[:, tb, ds(p * 512, 512)]
                                nc.vector.tensor_tensor(here, here, bank[tb][:, :], ALU.add).then_inc(o_h, 1)

                        def body(it, p):
                            for u in range(UN):
                                st.split_lo(dve, it, u, 2048)
                                if p is not None and u == 0:
                                    residual(p)
                        body(0, None)
                        body(1, 0)
                        with dve.Fori(2, N_IT) as it:
                            body(it, it - 1)
                        residual(N_IT - 1)

                    @block.tensor
                    def _(pe):
                        for k in range(KD):
                            if k >= 8:
                                pe.wait_ge(o_lo, 2 * (k // 2 - 4) + 2)
                            for tb in range(TB):
                                at = (k % 2) * T + tb * P
                                last = nc.tensor.transpose(bank[2 + (k // 2) % 4][:, at:at + P],
                                                           acc[:, tb, k * P:(k + 1) * P], ident[:, :])
                            last.then_inc(o_tr, 1)
                        pe.wait_ge(o_lo, KD)

                        def body(it, first):
                            if not first:
                                pe.wait_ge(o_h, TB * it)
                            for u in range(UN):
                                st.wait_unit(pe, it, u)
                                for kk in range(4):
                                    k = 4 * u + kk
                                    at = slice(kk * 512, (kk + 1) * 512)
                                    for tb in range(TB):
                                        t = slice(tb * P, (tb + 1) * P)
                                        last = tri_matmul(bank[tb][:, :], (yT_hi[:, k, t], yT_lo[:, k, t]),
                                                          (st.hi[u % st.split][:, at], st.lo[u % st.split][:, at]),
                                                          start=k == 0, stop=k == KD - 1)
                                last.then_inc(st.unit_used, 1)
                        body(0, True)
                        with pe.Fori(1, N_IT) as it:
                            body(it, False)

        nc.clear_and_free_semaphores([h.num for h in live])
        nc.all_engine_barrier()
        live.clear()

        rte = ExitStack()
        with rte:
            keysT = sb(rte, "keysT", [P, 2 * PH, PN])
            c = ExitStack()
            with c:
                hn = sb(c, "f_hn", [P, TB, D])
                keys = sb(c, "f_keys", [P, 2 * PH, P])
                junk = sb(c, "f_junk", [P, D])
                ssq = sb(c, "f_ssq", [P, TB])
                std = sb(c, "f_std", [P, TB])
                rstd = sb(c, "f_rstd", [P, TB])
                f_in = sem("f_in")
                f_ssq = sem("f_ssq")
                f_std = sem("f_std")
                f_rstd = sem("f_rstd")
                f_scaled = sem("f_scaled")
                f_xT = sem("f_xT")
                f_hi = sem("f_hi")
                f_lo = sem("f_lo")
                f_keys = sem("f_keysT")
                f_spill = sem("f_spill")
                f_kc = sem("f_kc")
                with nc.Block() as block:
                    @block.sync
                    def _(sp):
                        sp.dma_start(keys[:, :, :], peer_sub_keys[0].rearrange("h c n d -> n (h c) d")).then_inc(f_in, 16)
                        for tb in range(TB):
                            sp.dma_start(h_dram[tb * P:(tb + 1) * P, :], acc[:, tb, :]).then_inc(f_spill, 16)
                        sp.wait_ge(f_spill, 16 * TB)

                    @block.scalar
                    def _(act):
                        for tb in range(TB):
                            if tb:
                                act.wait_ge(f_ssq, tb)
                            nc.scalar.activation(junk[:, :], acc[:, tb, :], ACT.Square,
                                                 accum_out=ssq[:, tb:tb + 1]).then_inc(f_ssq, 1)
                        act.wait_ge(f_ssq, TB)
                        nc.scalar.activation(std[:, :], ssq[:, :], ACT.Sqrt, bias=eps_col[:, 0:1],
                                             scale=1.0 / D).then_inc(f_std, 1)
                        for k in range(KD):
                            act.wait_ge(f_xT, 2 * (k // 2) + 2)
                            nc.scalar.activation(xT_hi[:, k, :], bank[(k // 2) % 4][:, (k % 2) * T:(k % 2 + 1) * T],
                                                 ACT.Copy, scale=vcols[:, V_FFN + k:V_FFN + k + 1]).then_inc(f_hi, 1)
                        for b in range(4):
                            act.wait_ge(f_keys, b + 1)
                            nc.scalar.activation(keysT[:, 4 * b:4 * b + 4, :],
                                                 bank[4 + b][:, :].rearrange("p (k n) -> p k n", k=4),
                                                 ACT.Copy).then_inc(f_kc, 1)

                    @block.vector
                    def _(dve):
                        dve.wait_ge(f_std, 1)
                        nc.vector.reciprocal(rstd[:, :], std[:, :]).then_inc(f_rstd, 1)
                        dve.wait_ge(f_rstd, 1)
                        for tb in range(TB):
                            nc.vector.tensor_scalar(hn[:, tb, :], acc[:, tb, :], rstd[:, tb:tb + 1], None,
                                                    ALU.mult).then_inc(f_scaled, 1)
                        for k in range(KD):
                            dve.wait_ge(f_hi, 2 * (k // 2) + 2)
                            nc.vector.scalar_tensor_tensor(
                                out=xT_lo[:, k, :], in0=bank[(k // 2) % 4][:, (k % 2) * T:(k % 2 + 1) * T],
                                scalar=vcols[:, V_FFN + k:V_FFN + k + 1], in1=xT_hi[:, k, :].bitcast(F32),
                                op0=ALU.mult, op1=ALU.subtract).then_inc(f_lo, 1)

                    @block.tensor
                    def _(pe):
                        pe.wait_ge(f_in, 16)
                        for b in range(4):
                            for j in range(4):
                                last = nc.tensor.transpose(bank[4 + b][:, j * P:(j + 1) * P],
                                                           keys[:, 4 * b + j, :], ident[:, :])
                            last.then_inc(f_keys, 1)
                        pe.wait_ge(f_scaled, TB)
                        for k in range(KD):
                            if k >= 8:
                                pe.wait_ge(f_lo, 2 * (k // 2 - 4) + 2)
                            for tb in range(TB):
                                at = (k % 2) * T + tb * P
                                last = nc.tensor.transpose(bank[(k // 2) % 4][:, at:at + P],
                                                           hn[:, tb, k * P:(k + 1) * P], ident[:, :])
                            last.then_inc(f_xT, 1)

            qT = sb(rte, "qT", [P, 2 * PH, T])
            scores = sb(rte, "scores", [P, TB, 2 * PH, PN])
            c = ExitStack()
            with c:
                UN, N_IT = 4, D // 512
                st = Stream(c, "q", 4 * 512, UN, 2)
                q_c0 = sem("q_copied0")
                q_c1 = sem("q_copied1")
                q_s = sem("q_scores")
                q_sc = sem("q_scores_copied")
                with nc.Block() as block:
                    @block.sync
                    def _(sp):
                        def body(it, first):
                            for u in range(UN):
                                raw = st.raw[u][:, :].rearrange("p (k n) -> p k n", k=4)
                                st.load(sp, it, u, first, [
                                    (raw[:, half * 2:half * 2 + 2, :],
                                     peer_w_query[0, u * 512 + half * 256:u * 512 + half * 256 + 256,
                                                  ds(it * 512, 512)].rearrange("(k p) n -> p k n", p=P))
                                    for half in (1, 0)])
                        body(0, True)
                        with sp.Fori(1, N_IT) as it:
                            body(it, False)

                    @block.scalar
                    def _(act):
                        def copy(p):
                            act.wait_ge(st.unit_used, UN * p + UN)
                            nc.scalar.activation(qT[:, ds(4 * p, 2), :],
                                                 bank[0][:, :].rearrange("p (j t) -> p j t", j=2),
                                                 ACT.Copy).then_inc(q_c0, 1)

                        def body(it, p):
                            for u in range(UN):
                                st.split_hi(act, it, u, p is None, 2048)
                                if p is not None and u == 0:
                                    copy(p)
                        body(0, None)
                        with act.Fori(1, N_IT) as it:
                            body(it, it - 1)
                        copy(N_IT - 1)
                        for i in (0, 2, 4, 6):
                            act.wait_ge(q_s, i + 1)
                            nc.scalar.activation(scores[:, i // 4, 4 * (i % 4):4 * (i % 4) + 4, :],
                                                 bank[i][:, :].rearrange("p (k n) -> p k n", k=4),
                                                 ACT.Copy).then_inc(q_sc, 1)

                    @block.vector
                    def _(dve):
                        def copy(p):
                            dve.wait_ge(st.unit_used, UN * p + UN)
                            nc.vector.tensor_copy(qT[:, ds(4 * p + 2, 2), :],
                                                  bank[1][:, :].rearrange("p (j t) -> p j t", j=2)).then_inc(q_c1, 1)

                        def body(it, p):
                            for u in range(UN):
                                st.split_lo(dve, it, u, 2048)
                                if p is not None and u == 0:
                                    copy(p)
                        body(0, None)
                        with dve.Fori(1, N_IT) as it:
                            body(it, it - 1)
                        copy(N_IT - 1)
                        for i in (1, 3, 5, 7):
                            dve.wait_ge(q_s, i + 1)
                            nc.vector.tensor_copy(scores[:, i // 4, 4 * (i % 4):4 * (i % 4) + 4, :],
                                                  bank[i][:, :].rearrange("p (k n) -> p k n", k=4)).then_inc(q_sc, 1)

                    @block.tensor
                    def _(pe):
                        def body(it, first):
                            if not first:
                                pe.wait_ge(q_c0, it)
                                pe.wait_ge(q_c1, it)
                            for u in range(UN):
                                st.wait_unit(pe, it, u)
                                for kk in range(4):
                                    k = 4 * u + kk
                                    for m in range(4):
                                        at = slice(kk * 512 + m * P, kk * 512 + (m + 1) * P)
                                        last = tri_matmul(bank[m // 2][:, (m % 2) * T:(m % 2 + 1) * T],
                                                          (st.hi[u % st.split][:, at], st.lo[u % st.split][:, at]),
                                                          (xT_hi[:, k, :], xT_lo[:, k, :]),
                                                          start=k == 0 and m % 2 == 0, stop=k == KD - 1)
                                last.then_inc(st.unit_used, 1)
                        body(0, True)
                        with pe.Fori(1, N_IT) as it:
                            body(it, False)
                        pe.wait_ge(q_c0, N_IT)
                        pe.wait_ge(q_c1, N_IT)
                        for i in range(8):
                            tb, g = i // 4, i % 4
                            for j in range(4):
                                last = nc.tensor.matmul(bank[i][:, j * PN:(j + 1) * PN],
                                                        qT[:, 4 * g + j, tb * P:(tb + 1) * P], keysT[:, 4 * g + j, :],
                                                        start=True, stop=True)
                            last.then_inc(q_s, 1)

            c = ExitStack()
            with c:
                R, KEYS = TB * PH, 2 * TB * PH
                top_s = sb(c, "t_top_s", [P, KEYS, PK])
                top_i = sb(c, "t_top_i", [P, KEYS, PK], U32)
                key_f = sb(c, "t_key_f", [P, KEYS, PK])
                left = sb(c, "t_left", [P, KEYS, PN])
                cand = sb(c, "t_cand", [P, R, PK * PK])
                cand2 = sb(c, "t_cand2", [P, R, PK * PK])
                best = sb(c, "t_best", [P, R, PK])
                pos = sb(c, "t_pos", [P, R, PK], U32)
                side_u = sb(c, "t_side_u", [P, 2, R * PK], U32)
                side_f = sb(c, "t_side_f", [P, 2, R * PK])
                iota_u = sb(c, "t_iota_u", [P, PK], U32)
                iota_f = sb(c, "t_iota_f", [P, PK])
                diff = sb(c, "t_diff", [P, R, PK])
                expd = sb(c, "t_expd", [P, R, PK])
                total = sb(c, "t_total", [P, R])
                inv = sb(c, "t_inv", [P, R])
                t_step = sem("t_step")
                t_iota = sem("t_iota")
                t_max = sem("t_max")
                t_idx = sem("t_idx")
                t_rep = sem("t_rep")
                t_diff = sem("t_diff_done")
                t_exp = sem("t_exp")
                with nc.Block() as block:
                    @block.gpsimd
                    def _(pool):
                        pool.iota(iota_u[:, :], pattern=[[1, PK]], base=0, channel_multiplier=0).then_inc(t_iota, 1)

                    @block.scalar
                    def _(act):
                        act.wait_ge(t_diff, 1)
                        nc.scalar.activation(expd[:, :, :], diff[:, :, :], ACT.Exp).then_inc(t_exp, 1)

                    @block.vector
                    def _(dve):
                        v = nc.vector
                        flat = lambda a: a[:, :, :].rearrange("p a b -> p (a b)")

                        def sixteen(n, vals, rest, out_s, out_i, base):
                            for r in range(n):
                                v.max(out_s[:, r, 0:8], vals(r)).then_inc(t_max, 1)
                            for r in range(n):
                                dve.wait_ge(t_max, base[0] + r + 1)
                                v.max_index(out_i[:, r, 0:8], out_s[:, r, 0:8], vals(r)).then_inc(t_idx, 1)
                                v.match_replace(rest[:, r, :], out_s[:, r, 0:8], vals(r), -3.0e38).then_inc(t_rep, 1)
                            for r in range(n):
                                dve.wait_ge(t_rep, base[1] + r + 1)
                                v.max(out_s[:, r, 8:16], rest[:, r, :]).then_inc(t_max, 1)
                            for r in range(n):
                                dve.wait_ge(t_max, base[0] + n + r + 1)
                                v.max_index(out_i[:, r, 8:16], out_s[:, r, 8:16], rest[:, r, :]).then_inc(t_idx, 1)

                        sixteen(KEYS, lambda r: scores[:, r // (2 * PH), r % (2 * PH), :], left, top_s, top_i, (0, 0))
                        dve.wait_ge(t_idx, 2 * KEYS)
                        v.tensor_copy(flat(key_f), flat(top_i)).then_inc(t_step, 1)
                        sides = top_s[:, :, :].rearrange("p (r s) k -> p r s k", s=2)
                        for r in range(R):
                            v.tensor_tensor(cand[:, r, :].rearrange("p (a b) -> p a b", a=PK),
                                            sides[:, r, 0, :].unsqueeze(2).to_broadcast([P, PK, PK]),
                                            sides[:, r, 1, :].unsqueeze(1).to_broadcast([P, PK, PK]),
                                            ALU.add).then_inc(t_step, 1)
                        dve.wait_ge(t_step, 1 + R)
                        sixteen(R, lambda r: cand[:, r, :], cand2, best, pos, (2 * KEYS, KEYS))

                        v.tensor_tensor(diff[:, :, :], best[:, :, :], best[:, :, 0:1].to_broadcast([P, R, PK]),
                                        ALU.subtract).then_inc(t_diff, 1)
                        dve.wait_ge(t_idx, 2 * KEYS + 2 * R)
                        v.tensor_single_scalar(side_u[:, 0, :], flat(pos), 4, ALU.logical_shift_right).then_inc(t_step, 1)
                        v.tensor_single_scalar(side_u[:, 1, :], flat(pos), 15, ALU.bitwise_and).then_inc(t_step, 1)
                        dve.wait_ge(t_iota, 1)
                        v.tensor_copy(iota_f[:, :], iota_u[:, :]).then_inc(t_step, 1)
                        dve.wait_ge(t_step, R + 4)
                        v.tensor_copy(side_f[:, :, :], side_u[:, :, :]).then_inc(t_step, 1)
                        n = R + 5
                        keys_of = key_f[:, :, :].rearrange("p (r s) k -> p r s k", s=2)
                        for side in range(2):
                            hit = (cand, cand2)[side]
                            hit4 = hit[:, :, :].rearrange("p r (k a) -> p r k a", k=PK)
                            place = side_f[:, side, :].rearrange("p (r k) -> p r k", r=R)
                            dve.wait_ge(t_step, R + 5)
                            for r in range(R):
                                v.tensor_tensor(hit4[:, r], place[:, r, :].unsqueeze(2).to_broadcast([P, PK, PK]),
                                                iota_f[:, :].unsqueeze(1).to_broadcast([P, PK, PK]),
                                                ALU.is_equal).then_inc(t_step, 1)
                            for r in range(R):
                                dve.wait_ge(t_step, n + r + 1)
                                v.tensor_tensor(hit4[:, r], hit4[:, r],
                                                keys_of[:, r, side, :].unsqueeze(1).to_broadcast([P, PK, PK]),
                                                ALU.mult).then_inc(t_step, 1)
                            dve.wait_ge(t_step, n + 2 * R)
                            v.tensor_reduce(key_of[:, side, :],
                                            hit[:, :, :].rearrange("p r (k a) -> p (r k) a", k=PK),
                                            AX.X, ALU.add).then_inc(t_step, 1)
                            n += 2 * R + 1
                        dve.wait_ge(t_exp, 1)
                        v.tensor_reduce(total[:, :], expd[:, :, :], AX.X, ALU.add).then_inc(t_step, 1)
                        dve.wait_ge(t_step, n + 1)
                        v.reciprocal(inv[:, :], total[:, :]).then_inc(t_step, 1)
                        dve.wait_ge(t_step, n + 2)
                        v.tensor_tensor(gates[:, :, :].rearrange("p t (h k) -> p (t h) k", h=PH), expd[:, :, :],
                                        inv[:, :].unsqueeze(2).to_broadcast([P, R, PK]), ALU.mult).then_inc(t_step, 1)


        trunk.close()

        dense = ExitStack()
        with dense:
            coef = sb(dense, "coef", [P, PN, T])
            c = ExitStack()
            with c:
                NT = 16
                chosenT = sb(c, "m_chosenT", [P, 3, T])
                iota_u = sb(c, "m_iota_u", [P, PN], U32)
                iota_f = sb(c, "m_iota_f", [P, PN])
                first = sb(c, "m_first", [P, NT, PN])
                second = sb(c, "m_second", [P, NT, PN])
                m_iota = sem("m_iota")
                m_tr = sem("m_transposed")
                m_ready = sem("m_ready")
                m_first = sem("m_first")
                m_hot = sem("m_hot")
                m_second = sem("m_second")
                m_mm = sem("m_mm")
                m_out = sem("m_out")
                with nc.Block() as block:
                    @block.gpsimd
                    def _(pool):
                        pool.iota(iota_u[:, :], pattern=[[1, PN]], base=0, channel_multiplier=0).then_inc(m_iota, 1)
                        pool.wait_ge(m_ready, 4)

                        def body(it):
                            for b in range(4):
                                pool.wait_ge(m_hot, 4 * it + b + 1)
                                here = second[:, 4 * b:4 * b + 4, :]
                                pool.tensor_tensor(here, here,
                                                   chosenT[:, 2, ds(NT * it + 4 * b, 4)].unsqueeze(2).to_broadcast([P, 4, PN]),
                                                   ALU.mult).then_inc(m_second, 1)
                        with pool.Fori(0, T // NT) as it:
                            body(it)

                    @block.vector
                    def _(dve):
                        dve.wait_ge(m_iota, 1)
                        nc.vector.tensor_copy(iota_f[:, :], iota_u[:, :]).then_inc(m_ready, 1)
                        dve.wait_ge(m_tr, 1)
                        for i in range(3):
                            nc.vector.tensor_copy(chosenT[:, i, :], bank[i][:, 0:T]).then_inc(m_ready, 1)
                        dve.wait_ge(m_ready, 4)

                        def body(it, start):
                            for b in range(4):
                                if not start:
                                    dve.wait_ge(m_mm, NT * it - NT + 4 * b + 4)
                                four = slice(4 * b, 4 * b + 4)
                                for hot, row, done in ((second, 1, m_hot), (first, 0, m_first)):
                                    nc.vector.tensor_tensor(
                                        hot[:, four, :], iota_f[:, :].unsqueeze(1).to_broadcast([P, 4, PN]),
                                        chosenT[:, row, ds(NT * it + 4 * b, 4)].unsqueeze(2).to_broadcast([P, 4, PN]),
                                        ALU.is_equal).then_inc(done, 1)
                        body(0, True)
                        with dve.Fori(1, T // NT) as it:
                            body(it, False)

                    @block.tensor
                    def _(pe):
                        for i, src in enumerate((key_of[:, 0, :].rearrange("p (t n) -> p t n", t=TB),
                                                 key_of[:, 1, :].rearrange("p (t n) -> p t n", t=TB),
                                                 gates[:, :, :])):
                            for tb in range(TB):
                                last = nc.tensor.transpose(bank[i][:, tb * P:(tb + 1) * P], src[:, tb, :], ident[:, :])
                        last.then_inc(m_tr, 1)
                        pe.wait_ge(m_ready, 4)

                        def body(it, start):
                            for i in range(NT):
                                if i % 4 == 0:
                                    pe.wait_ge(m_first, 4 * it + i // 4 + 1)
                                    pe.wait_ge(m_second, 4 * it + i // 4 + 1)
                                if i % 4 == 0 and not start:
                                    pe.wait_ge(m_out, 4 * it - 4 + i // 4 + 1)
                                nc.tensor.matmul(bank[i // 4][:, (i % 4) * PN:(i % 4 + 1) * PN], first[:, i, :],
                                                 second[:, i, :], start=True, stop=True).then_inc(m_mm, 1)
                        body(0, True)
                        with pe.Fori(1, T // NT) as it:
                            body(it, False)

                    @block.scalar
                    def _(act):
                        with act.Fori(0, T // NT) as it:
                            for b in range(4):
                                act.wait_ge(m_mm, NT * it + 4 * b + 4)
                                nc.scalar.activation(
                                    coef[:, :, ds(NT * it + 4 * b, 4)].rearrange("p j t -> p t j"),
                                    bank[b][:, :].rearrange("p (t j) -> p t j", t=4), ACT.Copy).then_inc(m_out, 1)

            c = ExitStack()
            with c:
                HALF = D // 2
                raw = [sb(c, f"e_raw{i}", [P, HALF]) for i in range(4)]
                t_hi = [sb(c, f"e_hi{i}", [P, 4, P], F32R) for i in range(4)]
                t_lo = [sb(c, f"e_lo{i}", [P, 4, P], F32R) for i in range(4)]
                gel = [sb(c, f"e_gelu{i}", [P, T]) for i in range(2)]
                e_full = [sem(f"e_full{i}") for i in range(4)]
                e_tr = sem("e_turned")
                e_hi = sem("e_hi_done")
                e_lo = sem("e_lo_done")
                e_mm = sem("e_products")
                e_gelu = sem("e_gelu_done")
                e_coef = sem("e_coef")
                N_IT = PN // 2
                rows = peer_down[0].rearrange("(i j) d -> i j d", j=PN)
                prod = (bank[4], bank[5])
                with nc.Block() as block:
                    @block.sync
                    def _(sp):
                        def body(it, first):
                            for s_ in (1, 0, 3, 2):
                                if not first:
                                    sp.wait_ge(e_tr, 8 * it - 8 + 2 * s_ + 2)
                                for a, b in ((512, 1024), (0, 512)) if s_ % 2 == 0 else ((0, 1024),):
                                    sp.dma_start(raw[s_][:, a:b].rearrange("p (o d) -> p o d", o=1),
                                                 rows[:, ds(2 * it + s_ // 2, 1),
                                                      (s_ % 2) * HALF + a:(s_ % 2) * HALF + b]).then_inc(e_full[s_], 16)
                        body(0, True)
                        with sp.Fori(1, N_IT) as it:
                            body(it, False)

                    @block.tensor
                    def _(pe):
                        def turn(it, q, first):
                            if q % 2 == 0:
                                pe.wait_ge(e_full[q // 2], (it + 1) * (32 if q % 4 == 0 else 16))
                            if not (first and q < 4):
                                pe.wait_ge(e_lo, 8 * it + q - 3)
                            for b in range(4):
                                at = ((q % 2) * 4 + b) * P
                                last = nc.tensor.transpose(bank[q % 4][:, b * P:(b + 1) * P],
                                                           raw[q // 2][:, at:at + P], ident[:, :])
                            last.then_inc(e_tr, 1)

                        def products(it, q, first):
                            pe.wait_ge(e_lo, 8 * it + q + 1)
                            if q % 4 == 0 and not first:
                                pe.wait_ge(e_gelu, 2 * it - 1 + q // 4)
                            for b in range(4):
                                k = 4 * (q % 4) + b
                                last = tri_matmul(prod[q // 4][:, 0:T], (t_hi[q % 4][:, b, :], t_lo[q % 4][:, b, :]),
                                                  (xT_hi[:, k, :], xT_lo[:, k, :]), start=k == 0, stop=k == KD - 1)
                            last.then_inc(e_mm, 1)

                        def body(it, first, last):
                            for q in range(8):
                                if q < 6:
                                    turn(it, q + 2, first)
                                elif not last:
                                    turn(it + 1, q - 6, False)
                                products(it, q, first)
                        turn(0, 0, True)
                        turn(0, 1, True)
                        body(0, True, False)
                        with pe.Fori(1, N_IT - 1) as it:
                            body(it, False, False)
                        body(N_IT - 1, False, True)

                    @block.scalar
                    def _(act):
                        def hi(it, q, first):
                            act.wait_ge(e_tr, 8 * it + q + 1)
                            if not (first and q < 4):
                                act.wait_ge(e_mm, 8 * it + q - 3)
                            nc.scalar.activation(t_hi[q % 4][:, :, :], bank[q % 4][:, :].rearrange("p (b e) -> p b e", b=4),
                                                 ACT.Copy).then_inc(e_hi, 1)

                        def gelu(it, j, first):
                            act.wait_ge(e_mm, 8 * it + 4 * j + 4)
                            if not first:
                                act.wait_ge(e_coef, 2 * it + j - 1)
                            nc.scalar.activation(gel[j][:, :], prod[j][:, 0:T], ACT.Gelu).then_inc(e_gelu, 1)

                        def body(it, first, second):
                            for q in range(8):
                                hi(it, q, first)
                                if q == 2 and not first:
                                    gelu(it - 1, 1, second)
                                if q == 6:
                                    gelu(it, 0, first)
                        body(0, True, False)
                        body(1, False, True)
                        with act.Fori(2, N_IT) as it:
                            body(it, False, False)
                        gelu(N_IT - 1, 1, False)

                    @block.vector
                    def _(dve):
                        def lo(it, q):
                            dve.wait_ge(e_hi, 8 * it + q + 1)
                            nc.vector.tensor_tensor(t_lo[q % 4][:, :, :], bank[q % 4][:, :].rearrange("p (b e) -> p b e", b=4),
                                                    t_hi[q % 4][:, :, :].bitcast(F32), ALU.subtract).then_inc(e_lo, 1)

                        def weigh(it, j):
                            dve.wait_ge(e_gelu, 2 * it + j + 1)
                            here = coef[:, ds(2 * it + j, 1), :].rearrange("p o t -> p (o t)")
                            nc.vector.tensor_tensor(here, here, gel[j][:, :], ALU.mult).then_inc(e_coef, 1)

                        def body(it, first):
                            for q in range(8):
                                lo(it, q)
                                if q == 3 and not first:
                                    weigh(it - 1, 1)
                                if q == 7:
                                    weigh(it, 0)
                        body(0, True)
                        with dve.Fori(1, N_IT) as it:
                            body(it, False)
                        weigh(N_IT - 1, 1)

            c = ExitStack()
            with c:
                UN, N_IT, HALF = 8, PN // 4, D // 2
                st = Stream(c, "u", HALF, UN, (2, 1, 2, 1))
                cf_hi = [sb(c, f"u_coef_hi{i}", [P, T], F32R) for i in range(2)]
                cf_lo = [sb(c, f"u_coef_lo{i}", [P, T], F32R) for i in range(2)]
                u_hi = sem("u_coef_hi_done")
                u_lo = sem("u_coef_lo_done")
                rows = peer_up[0].rearrange("(i j) d -> i j d", j=PN)
                with nc.Block() as block:
                    @block.sync
                    def _(sp):
                        def body(it, first):
                            for u in range(UN):
                                at = (u % 2) * HALF
                                st.load(sp, it, u, first, [
                                    (st.raw[u % 4][:, a:b].rearrange("p (o d) -> p o d", o=1),
                                     rows[:, ds(4 * it + u // 2, 1), at + a:at + b])
                                    for a, b in (((512, 1024), (0, 512)) if u % 2 == 0 else ((0, 1024),))])
                        body(0, True)
                        with sp.Fori(1, N_IT) as it:
                            body(it, False)

                    @block.scalar
                    def _(act):
                        def coef_hi(it, j):
                            nc.scalar.activation(cf_hi[j % 2][:, :],
                                                 coef[:, ds(4 * it + j, 1), :].rearrange("p o t -> p (o t)"),
                                                 ACT.Copy).then_inc(u_hi, 1)

                        def body(it, first, last):
                            for u in range(UN):
                                st.split_hi(act, it, u, first, HALF)
                                if u % 2 == 1 and not (last and u == UN - 1):
                                    coef_hi(it, u // 2 + 1)
                        coef_hi(0, 0)
                        body(0, True, False)
                        with act.Fori(1, N_IT - 1) as it:
                            body(it, False, False)
                        body(N_IT - 1, False, True)

                    @block.vector
                    def _(dve):
                        def coef_lo(it, j):
                            dve.wait_ge(u_hi, 4 * it + j + 1)
                            nc.vector.tensor_tensor(cf_lo[j % 2][:, :],
                                                    coef[:, ds(4 * it + j, 1), :].rearrange("p o t -> p (o t)"),
                                                    cf_hi[j % 2][:, :].bitcast(F32), ALU.subtract).then_inc(u_lo, 1)

                        def body(it, last):
                            for u in range(UN):
                                st.split_lo(dve, it, u, HALF)
                                if u % 2 == 1 and not (last and u == UN - 1):
                                    coef_lo(it, u // 2 + 1)
                        coef_lo(0, 0)
                        with dve.Fori(0, N_IT - 1) as it:
                            body(it, False)
                        body(N_IT - 1, True)

                    @block.tensor
                    def _(pe):
                        def body(it, first):
                            for u in range(UN):
                                if u % 2 == 0:
                                    pe.wait_ge(u_lo, 4 * it + u // 2 + 1)
                                st.wait_unit(pe, it, u)
                                cf = (cf_hi[u // 2 % 2], cf_lo[u // 2 % 2])
                                for tb in range(TB):
                                    t = slice(tb * P, (tb + 1) * P)
                                    for cc in range(2):
                                        at = slice(cc * 512, (cc + 1) * 512)
                                        last = tri_matmul(bank[4 * tb + 2 * (u % 2) + cc][:, :], (cf[0][:, t], cf[1][:, t]),
                                                          (st.hi[u % 2][:, at], st.lo[u % 2][:, at]),
                                                          start=first and u < 2, stop=True)
                                last.then_inc(st.unit_used, 1)
                        body(0, True)
                        with pe.Fori(1, N_IT) as it:
                            body(it, False)

        c = ExitStack()
        with c:
            h = sb(c, "z_h", [P, TB, D])
            wide = sb(c, "z_wide", [P, D])
            junk = sb(c, "z_junk", [P, D])
            result = sb(c, "z_result", [P, TB, D])
            ssq = sb(c, "z_ssq", [P, TB])
            std = sb(c, "z_std", [P, TB])
            rstd = sb(c, "z_rstd", [P, TB])
            z_h = [sem(f"z_h_in{i}") for i in range(TB)]
            z_w = sem("z_wide_in")
            z_sum = sem("z_sum")
            z_ssq = sem("z_ssq")
            z_std = sem("z_std")
            z_rstd = sem("z_rstd")
            z_norm = sem("z_norm")
            z_out = sem("z_out")
            with nc.Block() as block:
                @block.sync
                def _(sp):
                    for tb in range(TB):
                        sp.dma_start(h[:, tb, :], h_dram[tb * P:(tb + 1) * P, :]).then_inc(z_h[tb], 16)
                    sp.dma_start(wide[:, :], final_norm_w.rearrange("(o d) -> o d", o=1).to_broadcast([P, D])).then_inc(z_w, 16)
                    for tb in range(TB):
                        sp.wait_ge(z_norm, tb + 1)
                        sp.dma_start(out[0, tb * P:(tb + 1) * P, :], result[:, tb, :]).then_inc(z_out, 16)
                    sp.wait_ge(z_out, 16 * TB)

                @block.vector
                def _(dve):
                    for tb in range(TB):
                        dve.wait_ge(z_h[tb], 16)
                        for cc in range(4):
                            here = h[:, tb, cc * 512:(cc + 1) * 512]
                            nc.vector.tensor_tensor(here, here, bank[4 * tb + cc][:, :], ALU.add).then_inc(z_sum, 1)
                    for tb in range(TB):
                        dve.wait_ge(z_std, tb + 1)
                        nc.vector.reciprocal(rstd[:, tb:tb + 1], std[:, tb:tb + 1]).then_inc(z_rstd, 1)
                        dve.wait_ge(z_rstd, tb + 1)
                        dve.wait_ge(z_w, 16)
                        nc.vector.scalar_tensor_tensor(out=result[:, tb, :], in0=h[:, tb, :],
                                                       scalar=rstd[:, tb:tb + 1], in1=wide[:, :],
                                                       op0=ALU.mult, op1=ALU.mult).then_inc(z_norm, 1)

                @block.scalar
                def _(act):
                    for tb in range(TB):
                        act.wait_ge(z_sum, 4 * tb + 4)
                        if tb:
                            act.wait_ge(z_std, tb)
                        nc.scalar.activation(junk[:, :], h[:, tb, :], ACT.Square,
                                             accum_out=ssq[:, tb:tb + 1]).then_inc(z_ssq, 1)
                        act.wait_ge(z_ssq, tb + 1)
                        nc.scalar.activation(std[:, tb:tb + 1], ssq[:, tb:tb + 1], ACT.Sqrt,
                                             bias=eps_col[:, 0:1], scale=1.0 / D).then_inc(z_std, 1)




_INS = ['x', 'norm_mix_w', 'w_in', 'conv_a_w', 'ssd_conv_w', 'ssd_conv_b', 'ssd_dt_bias', 'ssd_a_log', 'ssd_d',
        'ssd_norm_w', 'w_branch_a', 'w_branch_b', 'w_branch_c', 'w_out', 'norm_ffn_w', 'peer_w_query',
        'peer_sub_keys', 'peer_down', 'peer_up', 'final_norm_w']


def kernel(**inputs):
    import concourse.bacc as bacc
    from concourse.bass_utils import run_bass_kernel_spmd

    nc = bacc.Bacc("TRN2", target_bir_lowering=False, num_devices=1)
    arrays, args = {}, []
    for name in _INS:
        a = np.ascontiguousarray(inputs[name])
        arrays[f"in_{name}"] = a
        args.append(nc.dram_tensor(f"in_{name}", a.shape, mybir.dt.from_np(a.dtype), kind="ExternalInput").ap())
    args.append(nc.dram_tensor("h_scratch", (T, D), F32, kind="Internal").ap())
    args.append(nc.dram_tensor("out_0", (1, T, D), F32, kind="ExternalOutput").ap())
    program(nc, *args)
    return run_bass_kernel_spmd(nc, [arrays], core_ids=[0]).results[0]["out_0"]
```
